# Optimizing a Trainium2 kernel written in Bass

```python
import jax, jax.numpy as jnp
from jax import lax
import numpy as np

D_MODEL = 1024
BATCH = 1
SEQ = 1024
DEPTH = 1

CHUNK = 64
CONV_DIM = 512
CONV_GROUPS = 8
CONV_WIDTH = 31
N_HEADS = 8
N_KV_HEADS = 2
HEAD_DIM = 64
GQA = N_HEADS // N_KV_HEADS
Q_DIM = N_HEADS * HEAD_DIM
KV_DIM = N_KV_HEADS * HEAD_DIM
MIX_DIM = CONV_DIM + Q_DIM
IN_DIM = 2 * CONV_DIM + Q_DIM + 2 * KV_DIM
WINDOW = 128
WINDOW_CHUNKS = WINDOW // CHUNK
BAND = WINDOW_CHUNKS * CHUNK
D_FF = 2816
N_SUB = 3
RES_WEIGHTS = (0.5, 1.0, 0.5)
EPS = 1e-6
NEG_INF = -1e30

kernel_name = "hymba_conformer_swa_sink_alibi_macaron"

def rms_norm(x, g):
    xf = x.astype(jnp.float32)
    y = xf * lax.rsqrt(jnp.mean(xf * xf, axis=-1, keepdims=True) + EPS)
    return (y * g.astype(jnp.float32)).astype(x.dtype)

def layer_norm(x, g, b):
    xf = x.astype(jnp.float32)
    mu = jnp.mean(xf, axis=-1, keepdims=True)
    xc = xf - mu
    y = xc * lax.rsqrt(jnp.mean(xc * xc, axis=-1, keepdims=True) + EPS)
    return (y * g.astype(jnp.float32) + b.astype(jnp.float32)).astype(x.dtype)

def swiglu(h, w_gate, w_up, w_down):
    return (jax.nn.silu(h @ w_gate) * (h @ w_up)) @ w_down

def conformer_conv(u_a, u_b, w_dw, b_dw, ln_g, ln_b):
    u = u_a * jax.nn.sigmoid(u_b)
    y = lax.conv_general_dilated(
        u, w_dw.astype(u.dtype), window_strides=(1,), padding=[(CONV_WIDTH - 1, 0)],
        dimension_numbers=("NWC", "WIO", "NWC"), feature_group_count=CONV_DIM)
    y = y + b_dw
    return jax.nn.silu(layer_norm(y, ln_g, ln_b))

def alibi_slopes():
    return jnp.exp2(-8.0 * jnp.arange(1, N_HEADS + 1, dtype=jnp.float32) / N_HEADS)

def chunk_band(t, n_chunks):
    pad = jnp.pad(t, ((0, 0), (WINDOW_CHUNKS - 1, 0), (0, 0), (0, 0), (0, 0)))
    return jnp.concatenate([pad[:, i:i + n_chunks] for i in range(WINDOW_CHUNKS)], axis=2)

def swa_sink_attention(q, k, v, sinks):
    B, S, _ = q.shape
    n_chunks = S // CHUNK
    q = q.reshape(B, n_chunks, CHUNK, N_KV_HEADS, GQA, HEAD_DIM)
    k = chunk_band(k.reshape(B, n_chunks, CHUNK, N_KV_HEADS, HEAD_DIM), n_chunks)
    v = chunk_band(v.reshape(B, n_chunks, CHUNK, N_KV_HEADS, HEAD_DIM), n_chunks)
    s = jnp.einsum("bnqkgd,bnskd->bnkgqs", q, k).astype(jnp.float32) * (HEAD_DIM ** -0.5)
    qi = jnp.arange(CHUNK)[:, None]
    kj = jnp.arange(BAND)[None, :]
    dist = jnp.abs(qi + (WINDOW_CHUNKS - 1) * CHUNK - kj).astype(jnp.float32)
    s = s - alibi_slopes().reshape(N_KV_HEADS, GQA, 1, 1) * dist
    valid = (jnp.arange(n_chunks)[:, None] - (WINDOW_CHUNKS - 1) + kj // CHUNK) >= 0
    s = jnp.where(valid[:, None, None, None, :], s, NEG_INF)
    sink = jnp.broadcast_to(sinks.astype(jnp.float32).reshape(N_KV_HEADS, GQA, 1, 1),
                            s.shape[:-1] + (1,))
    p = jax.nn.softmax(jnp.concatenate([s, sink], axis=-1), axis=-1)[..., :-1]
    o = jnp.einsum("bnkgqs,bnskd->bnqkgd", p.astype(v.dtype), v)
    return o.reshape(B, S, Q_DIM)

def token_mixer(h, w_in, conv_w, conv_b, conv_ln_g, conv_ln_b, sinks, w_out):
    z = h @ w_in
    o1 = CONV_DIM
    o2 = 2 * CONV_DIM
    o3 = o2 + Q_DIM
    o4 = o3 + KV_DIM
    conv_out = conformer_conv(z[..., :o1], z[..., o1:o2], conv_w, conv_b, conv_ln_g, conv_ln_b)
    attn_out = swa_sink_attention(z[..., o2:o3], z[..., o3:o4], z[..., o4:], sinks)
    return jnp.concatenate([conv_out, attn_out], axis=-1) @ w_out

def setup_inputs(seed: int = 0) -> dict:
    key = jax.random.key(seed)
    ks = jax.random.split(key, 20)
    f32 = jnp.float32

    def nrm(k, shape, fan_in):
        return jax.random.normal(k, shape, f32) * (fan_in ** -0.5)

    return {
        "x": jax.random.normal(ks[0], (BATCH, SEQ, D_MODEL), f32),
        "c": jax.random.normal(ks[1], (BATCH, D_MODEL), f32),
        "ada_w": nrm(ks[2], (DEPTH, D_MODEL, 3 * N_SUB * D_MODEL), D_MODEL),
        "ada_b": 0.01 * jax.random.normal(ks[3], (DEPTH, 3 * N_SUB * D_MODEL), f32),
        "norm_pre": 1.0 + 0.01 * jax.random.normal(ks[4], (DEPTH, N_SUB, D_MODEL), f32),
        "norm_post": 1.0 + 0.01 * jax.random.normal(ks[5], (DEPTH, N_SUB, D_MODEL), f32),
        "ffn1_w_gate": nrm(ks[6], (DEPTH, D_MODEL, D_FF), D_MODEL),
        "ffn1_w_up": nrm(ks[7], (DEPTH, D_MODEL, D_FF), D_MODEL),
        "ffn1_w_down": nrm(ks[8], (DEPTH, D_FF, D_MODEL), D_FF),
        "ffn2_w_gate": nrm(ks[9], (DEPTH, D_MODEL, D_FF), D_MODEL),
        "ffn2_w_up": nrm(ks[10], (DEPTH, D_MODEL, D_FF), D_MODEL),
        "ffn2_w_down": nrm(ks[11], (DEPTH, D_FF, D_MODEL), D_FF),
        "mix_w_in": nrm(ks[12], (DEPTH, D_MODEL, IN_DIM), D_MODEL),
        "conv_w": nrm(ks[13], (DEPTH, CONV_WIDTH, 1, CONV_DIM), CONV_WIDTH),
        "conv_b": 0.01 * jax.random.normal(ks[14], (DEPTH, CONV_DIM), f32),
        "conv_ln_g": 1.0 + 0.01 * jax.random.normal(ks[15], (DEPTH, CONV_DIM), f32),
        "conv_ln_b": 0.01 * jax.random.normal(ks[16], (DEPTH, CONV_DIM), f32),
        "attn_sinks": jax.random.normal(ks[17], (DEPTH, N_HEADS), f32),
        "mix_w_out": nrm(ks[18], (DEPTH, MIX_DIM, D_MODEL), MIX_DIM),
    }

def reference(x, c, ada_w, ada_b, norm_pre, norm_post,
              ffn1_w_gate, ffn1_w_up, ffn1_w_down,
              ffn2_w_gate, ffn2_w_up, ffn2_w_down,
              mix_w_in, conv_w, conv_b, conv_ln_g, conv_ln_b, attn_sinks, mix_w_out):
    B = x.shape[0]
    for l in range(DEPTH):
        mod = (jax.nn.silu(c) @ ada_w[l] + ada_b[l]).reshape(B, 3 * N_SUB, 1, D_MODEL)

        def sublayer(x, i, fn):
            shift, scale, gate = mod[:, 3 * i], mod[:, 3 * i + 1], mod[:, 3 * i + 2]
            h = rms_norm(x, norm_pre[l, i]) * (1.0 + scale) + shift
            return x + RES_WEIGHTS[i] * gate * rms_norm(fn(h), norm_post[l, i])

        x = sublayer(x, 0, lambda h: swiglu(h, ffn1_w_gate[l], ffn1_w_up[l], ffn1_w_down[l]))
        x = sublayer(x, 1, lambda h: token_mixer(h, mix_w_in[l], conv_w[l], conv_b[l],
                                                 conv_ln_g[l], conv_ln_b[l],
                                                 attn_sinks[l], mix_w_out[l]))
        x = sublayer(x, 2, lambda h: swiglu(h, ffn2_w_gate[l], ffn2_w_up[l], ffn2_w_down[l]))
    return x


_drawn_inputs = setup_inputs


def setup_inputs(seed=0):
    import zlib

    import numpy as np

    out = dict(_drawn_inputs(seed))
    spreads = {}
    factors = {'ada_b': 4.024,
     'norm_pre': 7.872,
     'norm_post': 8.0,
     'conv_b': 64.0,
     'conv_ln_g': 64.0,
     'conv_ln_b': 64.0,
     'attn_sinks': 8.0}
    for name, (base, spread) in spreads.items():
        noise = np.random.default_rng([zlib.crc32(name.encode()), seed]).standard_normal(out[name].shape)
        drawn = base * np.exp(spread * noise) if base else spread * noise
        out[name] = __import__('jax').numpy.asarray(drawn.astype(out[name].dtype))
    for name, factor in factors.items():
        out[name] = (out[name] * factor).astype(out[name].dtype)
    return out
```

```python
import concourse.bass as bass
from concourse import mybir
from contextlib import ExitStack


def layer(nc, x_in, c, ada_w, ada_b, norm_pre, norm_post,
          w_gate1, w_up1, w_down1, w_gate2, w_up2, w_down2,
          w_in, conv_w, conv_b, ln_g, ln_b, sinks, w_out, out):
    F32, F32R = mybir.dt.float32, mybir.dt.float32r
    ALU, ACT, AX = mybir.AluOpType, mybir.ActivationFunctionType, mybir.AxisListType

    P = 128
    S, D = x_in.shape[1], x_in.shape[2]
    KT = D // P
    HT = S // 2
    TT = HT // P
    FF = w_down1.shape[1]
    FG = 2
    NG = FF // (FG * P)
    CONV = conv_b.shape[1]
    CT = CONV // P
    TAPS = conv_w.shape[1]
    HIST = TAPS - 1
    NH = sinks.shape[1]
    HD = 64
    CH = 64
    NCH = S // CH
    QT = NH * HD // P
    NM = 9
    NB_D = D // 512
    EPS = 1e-6
    RES = (0.5, 1.0, 0.5)
    NEG = -1e30
    LAST = NG - 1
    G2 = NG

    x_tok = x_in[0].rearrange("(t p) d -> t p d", p=P)
    out_tok = out[0].rearrange("(t p) d -> t p d", p=P)
    ffn_w = ((w_gate1[0], w_up1[0], w_down1[0]), (w_gate2[0], w_up2[0], w_down2[0]))

    ctx = ExitStack()
    with ctx:
        def sb(name, shape, dt=F32):
            return ctx.enter_context(nc.sbuf_tensor(name, shape, dt))

        def sem(name):
            return ctx.enter_context(nc.semaphore(name))

        h_hi = sb("h_hi", [P, KT, S], F32R)
        h_lo = sb("h_lo", [P, KT, S], F32R)
        yreg = sb("yreg", [P, 2 * TT * D])
        y_ffn = yreg[:, :].rearrange("p (t d) -> p t d", d=D)
        gu_hi = sb("gu_hi", [P, 4, KT * P], F32R)
        gu_lo = sb("gu_lo", [P, 4, KT * P], F32R)
        dn_hi = sb("dn_hi", [P, FG, D], F32R)
        dn_lo = sb("dn_lo", [P, FG, D], F32R)
        act_hi = sb("act_hi", [P, 2, FG * HT], F32R)
        act_lo = sb("act_lo", [P, 2, FG * HT], F32R)
        raw = sb("raw", [P, 4, KT * P])
        xring = sb("xring", [P, 2, D])
        gate_b = sb("gate_b", [P, D])
        th = sb("th", [P, HT])
        a_full = sb("a_full", [P, HT])
        s01 = sb("s01", [P, 2, 512])
        pT = sb("pT", [P, 512])
        v_even = sb("v_even", [P, TT, P])
        ident = sb("ident", [P, P])
        ones = sb("ones", [P, P])
        vecs = sb("vecs", [P, 276])
        modcol = sb("modcol", [P, NM, KT])
        amul = sb("amul", [P, 3, KT])
        gcol = sb("gcol", [P, 3, KT])
        silu_c = sb("silu_c", [P, KT])
        alibi = sb("alibi", [P, 2, 4, P])
        sink_col = sb("sink_col", [P, 4])
        eps_col = sb("eps_col", [P, 1])
        stat = sb("stat", [P, 16, 4])
        SSQ, ROOT, VAR, T1, T2, RSTDY, RSTDX = range(7)
        MX, NEGM, DIFF, SUMS, ES, DEN, RDEN = range(7, 14)

        o = 0
        u_buf = yreg[:, o:o + CT * (HIST + HT)].rearrange("p (c t) -> p c t", c=CT)
        o += CT * (HIST + HT)
        acc = yreg[:, o:o + CT * HT].rearrange("p (c t) -> p c t", c=CT)
        o += CT * HT
        q_buf = yreg[:, o:o + QT * HT].rearrange("p (n g t) -> p n g t", g=QT, t=CH)
        o += QT * HT
        k_buf = yreg[:, o:o + S]
        o += S
        v_odd = yreg[:, o:o + TT * P].rearrange("p (t d) -> p t d", t=TT)
        assert o + TT * P <= 2 * TT * D

        hf = [pT[:, :], v_even[:, :, :].rearrange("p t d -> p (t d)")]
        ada_acc = s01[:, :, :].rearrange("p a b -> p (a b)")
        diag = ada_acc

        def junk(e):
            return gate_b[:, :] if e < 2 else ada_acc

        vec_raw = pT
        ada_b_col = vecs[:, 0:NM * KT].rearrange("p (m j) -> p m j", j=KT)
        npre_col = vecs[:, 72:96].rearrange("p (s j) -> p s j", j=KT)
        npost_col = vecs[:, 96:120].rearrange("p (s j) -> p s j", j=KT)
        taps_col = vecs[:, 128:128 + TAPS * CT].rearrange("p (t c) -> p t c", c=CT)
        c_col = vecs[:, 256:264]
        convb_col = vecs[:, 264:268]
        lng_col = vecs[:, 268:272]
        lnb_col = vecs[:, 272:276]

        bank = [ctx.enter_context(nc.psum_tensor(f"bank{i}", [P, 512], F32)) for i in range(8)]

        const_ready = sem("const_ready")
        vec_in = sem("vec_in")
        vec_mm = sem("vec_mm")
        vec_ready = sem("vec_ready")
        thc_done = sem("thc_done")
        x0_in = sem("x0_in")
        x0b_in = sem("x0b_in")
        ada_in = [sem(f"ada_in{i}") for i in range(6)]
        ada_used = sem("ada_used")
        ada_mm = sem("ada_mm")
        ada_col = sem("ada_col")
        amul_ready = sem("amul_ready")
        raw0_in = sem("raw0_in")
        raw1_in = sem("raw1_in")
        gu_hi_r, gu_lo_r = sem("gu_hi_r"), sem("gu_lo_r")
        dn_hi_r, dn_lo_r = sem("dn_hi_r"), sem("dn_lo_r")
        gate_mm, up_mm = sem("gate_mm"), sem("up_mm")
        th_done = sem("th_done")
        gate_free, up_free = sem("gate_free"), sem("up_free")
        act_hi_r, act_lo_r = sem("act_hi_r"), sem("act_lo_r")
        down_mm = sem("down_mm")
        y_done = sem("y_done")
        root_y, root_x = sem("root_y"), sem("root_x")
        x_tile_in = [sem(f"x_tile_in{i}") for i in range(2)]
        x1_ready = sem("x1_ready")
        x1_stored = [sem(f"x1_stored{i}") for i in range(4)]
        rstd_x = sem("rstd_x")
        xhat_r = sem("xhat_r")
        t_mm = sem("t_mm")
        hf_done = sem("hf_done")
        h_hi_r, h_lo_r = sem("h_hi_r"), sem("h_lo_r")
        diag_r = sem("diag_r")
        gb_mm = sem("gb_mm")
        gb_done = sem("gb_done")
        ring_in = [sem(f"ring_in{i}") for i in range(4)]
        ring_hi, ring_lo = sem("ring_hi"), sem("ring_lo")
        step_mm = sem("step_mm")
        step_act, step_dve = sem("step_act"), sem("step_dve")
        th_b = sem("th_b")
        vt_mm, vt_done = sem("vt_mm"), sem("vt_done")
        conv_done = sem("conv_done")
        mean_mm, cen_done = sem("mean_mm"), sem("cen_done")
        sq_done, var_mm = sem("sq_done"), sem("var_mm")
        lroot, ldiag = sem("lroot"), sem("ldiag")
        lb_mm = sem("lb_mm")
        yn_done = sem("yn_done")
        lth_done, lf_done = sem("lth_done"), sem("lf_done")
        c_hi_r, c_lo_r = sem("c_hi_r"), sem("c_lo_r")
        s_mm = sem("s_mm")
        s_read = sem("s_read")
        mx_r = sem("mx_r")
        p_r = sem("p_r")
        pn_r = sem("pn_r")
        pT_mm, pT_r = sem("pT_mm"), sem("pT_r")
        o_mm = sem("o_mm")
        o_hi_r, o_lo_r = sem("o_hi_r"), sem("o_lo_r")
        act_self, dve_self, pool_self = sem("act_self"), sem("dve_self"), sem("pool_self")

        class Chain:

            def __init__(self, eng, s):
                self.eng, self.s, self.n = eng, s, 0

            def __call__(self, ins):
                self.n += 1
                ins.then_inc(self.s, 1)
                self.eng.wait_ge(self.s, self.n)

            def mark(self, ins):
                self.n += 1
                ins.then_inc(self.s, 1)
                return self.n

        TILES = [t for j in range(CT) for t in (("b", j), ("a", j))] + [("k", 0), ("v", 0)] + \
                [("q", g) for g in range(QT)]
        NIN = len(TILES)
        NOUT = TT * NB_D
        OUT0 = 2 * NIN
        RING = []
        for i in range(2 * NIN):
            RING.append(("in", i))
            if i in (NIN, NIN + 2, NIN + 4, NIN + 6):
                RING.append(("out", 4 + (i - NIN) // 2))
        RING += [("out", kt) for kt in range(4)]
        IN_AT = {i: n for n, (kind, i) in enumerate(RING) if kind == "in"}
        OUT_AT = {i: n for n, (kind, i) in enumerate(RING) if kind == "out"}

        def ring_dmas(n):
            kind, i = RING[n]
            t = TILES[i % NIN][0] if kind == "in" else None
            return 2 if t == "q" or (kind == "out" and i >= 4) else 1

        RING_COUNT = []
        seen = [0] * 4
        for n in range(len(RING)):
            seen[n % 4] += 16 * ring_dmas(n)
            RING_COUNT.append(seen[n % 4])

        def ring_dst(n):
            kind, i = RING[n]
            if kind == "in":
                return gu_hi[:, i % 4, :], gu_lo[:, i % 4, :]
            return wout_tile(i)

        def wout_tile(kt):
            if kt < 4:
                return gu_hi[:, kt, :], gu_lo[:, kt, :]
            if kt < 6:
                return act_hi[:, kt - 4, :], act_lo[:, kt - 4, :]
            return dn_hi[:, kt - 6, :], dn_lo[:, kt - 6, :]

        def ring_upto(st):
            if st + 3 < 2 * NIN:
                return IN_AT[st + 3] + 1
            return min(len(RING), IN_AT[2 * NIN - 1] + 1 + (st + 3 - 2 * NIN) + 1)

        def is_dve_step(st):
            return st < OUT0 and TILES[st % NIN][0] == "a"

        def step_reads(st):
            if is_dve_step(st):
                return step_dve, sum(is_dve_step(i) for i in range(st + 1))
            return step_act, sum(not is_dve_step(i) for i in range(st + 1))

        V_STEP = [i for i, t in enumerate(TILES) if t[0] == "v"][0]
        VT_STEP = V_STEP + 1
        SLOT_STEP = [NIN + i for i in range(8)] + [OUT0 + i for i in range(8)]

        def slots(st):
            for half in (0, 1):
                base = (NIN, OUT0)[half]
                x = st - base
                if 0 <= x < 10:
                    return (8 * half + x if x < 8 else None,
                            8 * half + x - 1 if 1 <= x < 9 else None,
                            8 * half + x - 2 if x >= 2 else None)
            return (None, None, None)

        CONV_AT = {}
        for half, plan in ((0, [(0, 2, 6), (1, 8, 13), (2, 14, 18), (3, 19, 20)]),
                           (1, [(0, 24, 27), (1, 28, 30), (2, 31, 33), (3, 34, 35)])):
            for ct, first, last in plan:
                n = last - first + 1
                for k in range(n):
                    CONV_AT.setdefault(first + k, []).append(
                        (half, ct, k * TAPS // n, (k + 1) * TAPS // n))
        LN_STEP = (21, 35)
        GATEB_STEP = 8
        NORM_B = (0, 1, 2)
        TB_STEPS = (3, 4, 5, 6)
        TA_STEPS = (40, 41, 42, 43)
        assert TAPS == 31 and NIN == 14 and OUT0 == 28

        def post_y(e):
            if e in (2, 3, 6, 7):
                return [y_ffn[:, TT * (e % 2) + i, :] for i in range(TT)]
            if e == 4:
                return [raw[:, i, :] for i in range(TT)]
            return [y_ffn[:, TT + i, :] for i in range(TT)]

        def pre_x(e):
            return post_y(e) if e >= 2 else [y_ffn[:, TT * e + i, :] for i in range(TT)]

        def t_bank(e, j):
            return j % 4 if e == 2 else 4 + j % 4

        block = ctx.enter_context(nc.Block())

        @block.sync
        def _(sp):
            sp.dma_start(vec_raw[0:72, 0:P], ada_b[0].rearrange("(r p) -> r p", p=P)).then_inc(vec_in, 16)
            sp.dma_start(vec_raw[72:96, 0:P], norm_pre[0].rearrange("s (j p) -> (s j) p", p=P)).then_inc(vec_in, 16)
            sp.dma_start(vec_raw[96:120, 0:P], norm_post[0].rearrange("s (j p) -> (s j) p", p=P)).then_inc(vec_in, 16)
            sp.dma_start(vec_raw[0:TAPS * CT, P:2 * P], conv_w[0].rearrange("t o (c p) -> (t o c) p", p=P)).then_inc(vec_in, 16)
            sp.dma_start(vec_raw[0:8, 2 * P:3 * P], c.rearrange("b (j p) -> (b j) p", p=P)).then_inc(vec_in, 16)
            for n, v in enumerate((conv_b, ln_g, ln_b)):
                sp.dma_start(vec_raw[8 + 4 * n:12 + 4 * n, 2 * P:3 * P],
                             v.rearrange("b (j p) -> (b j) p", p=P)).then_inc(vec_in, 16)
            with nc.allow_non_contiguous_dma(reason="sinks of a head on its 64 rows"):
                for hh in range(2):
                    sp.dma_start(sink_col[64 * hh:64 * hh + 64, :],
                                 sinks.rearrange("a (i h) -> a h i", h=2)[:, hh, :].to_broadcast([64, 4])
                                 ).then_inc(vec_in, 16)

            def ada_row(m, kt):
                return ada_w[0, kt * P:(kt + 1) * P, bass.ds(m * D, D)]

            for n in range(2 * KT):
                m, kt = n // KT, n % KT
                if n >= 6:
                    sp.wait_ge(ada_used, n - 5)
                dst = raw[:, n % 6, :] if n % 6 < 4 else xring[:, n % 6 - 4, :]
                sp.dma_start(dst, ada_row(m, kt)).then_inc(ada_in[n % 6], 16)
                if n >= KT:
                    t = n - KT
                    sp.dma_start(y_ffn[:, t, :], x_tok[t]).then_inc(x0_in if t < TT else x0b_in, 16)

            def load_gu(s, g, which):
                w = ffn_w[s][which].rearrange("(k p) f -> p k f", p=P)
                dst = raw[:, 2 * which:2 * which + 2, :].rearrange("p a b -> p (a b)")
                dst = dst.rearrange("p (k f) -> p k f", k=KT)
                src = w[:, :, bass.ds(g * (FG * P), FG * P)]
                return dst, src, (raw0_in, raw1_in)[which]

            def load_dn(s, g):
                w = ffn_w[s][2][bass.ds(g * (FG * P), FG * P), :].rearrange("(f p) d -> p f d", p=P)
                return raw[:, 0:FG, :], w, raw0_in

            def start(x):
                dst, src, s = x
                sp.dma_start(dst, src).then_inc(s, 16)

            sp.wait_ge(ada_used, 2 * KT)
            start(load_gu(0, 0, 0))
            start(load_gu(0, 0, 1))

            def ffn_group(s, G, g, ada, last):
                dn = load_dn(s, g)
                if not last:
                    up, gate = load_gu(s, g + 1, 1), load_gu(s, g + 1, 0)
                sp.wait_ge(gu_lo_r, 4 * G + 4)
                start(dn)
                if not last:
                    start(up)
                if ada:
                    for kt in range(KT):
                        src = ada_row(g + 1, kt)
                        sp.wait_ge(ada_used, (g + 1) * KT + kt - 1)
                        sp.dma_start(xring[:, kt % 2, :], src).then_inc(ada_in[4 + kt % 2], 16)
                if not last:
                    sp.wait_ge(dn_lo_r, G + 1)
                    start(gate)

            def ffn(s, G0):
                ffn_group(s, G0, 0, False, False)
                if s == 0:
                    with sp.Fori(1, NM - 1) as g:
                        ffn_group(0, g, g, True, False)
                    with sp.Fori(NM - 1, LAST) as g:
                        ffn_group(0, g, g, False, False)
                else:
                    with sp.Fori(1, LAST) as g:
                        ffn_group(1, g + G2, g, False, False)
                ffn_group(s, G0 + LAST, LAST, False, True)

            def load_ring(n):
                kind, i = RING[n]
                dst = raw[:, n % 4, :]
                s = ring_in[n % 4]
                if kind == "in":
                    t, j = TILES[i % NIN]
                    wv = w_in[0].rearrange("(k p) n -> p k n", p=P)
                    dv = dst.rearrange("p (k n) -> p k n", k=KT)
                    if t == "q":
                        for kv in range(2):
                            col = 2 * CONV + (kv * QT + j) * HD
                            sp.dma_start(dv[:, :, kv * HD:(kv + 1) * HD], wv[:, :, col:col + HD]).then_inc(s, 16)
                    else:
                        col = {"a": j * P, "b": CONV + j * P, "k": 2 * CONV + NH * HD,
                               "v": 2 * CONV + NH * HD + P}[t]
                        sp.dma_start(dv, wv[:, :, col:col + P]).then_inc(s, 16)
                elif i < 4:
                    sp.dma_start(dst, w_out[0, i * P:(i + 1) * P, :]).then_inc(s, 16)
                else:
                    for kv in range(2):
                        row = CONV + (kv * QT + i - 4) * HD
                        sp.dma_start(dst[kv * HD:(kv + 1) * HD, :], w_out[0, row:row + HD, :]).then_inc(s, 16)

            ffn(0, 0)
            sp.wait_ge(dn_lo_r, LAST + 1)
            load_ring(0)
            load_ring(1)
            load_ring(2)
            load_ring(3)
            for n in range(4, len(RING)):
                sp.wait_ge(ring_lo, n - 3)
                load_ring(n)
            sp.wait_ge(t_mm, 8 * 5)
            start(load_gu(1, 0, 0))
            start(load_gu(1, 0, 1))
            ffn(1, G2)

        @block.gpsimd
        def _(pool):
            one = Chain(pool, pool_self)
            pool.memset(ones[:, :], 1.0)
            pool.memset(eps_col[:, :], EPS)
            one(pool.memset(ident[:, :], 0.0))
            one(pool.affine_select(out=ident[:, :], in_=ident[:, :], compare_op=ALU.not_equal, fill=1.0,
                                   base=0, pattern=[[-1, P]], channel_multiplier=1))
            for hh in range(2):
                pool.iota(s01[64 * hh:64 * hh + 64, 0, 0:P], pattern=[[-1, P]], base=CH, channel_multiplier=1,
                          allow_small_or_imprecise_dtypes=True).then_inc(const_ready, 1)

            xn = [0]

            def load_x(e, i):
                n = xn[0]
                xn[0] += 1
                if n >= 2:
                    pool.wait_ge(x1_ready, n - 1)
                src = x_tok[TT * (e % 2) + i] if e < 4 else out_tok[TT * (e % 2) + i]
                if e >= 4:
                    pool.wait_ge(x1_stored[i], 16 * (e - 3))
                pool.dma_start(xring[:, n % 2, :], src).then_inc(x_tile_in[n % 2], 16)

            def store_x(e, i):
                pool.wait_ge(x1_ready, 4 * (e - 2) + i + 1)
                pool.dma_start(out_tok[TT * (e % 2) + i], post_y(e)[i]).then_inc(x1_stored[i], 16)

            def post_dmas(e):
                load_x(e, 0)
                load_x(e, 1)
                for i in range(TT):
                    store_x(e, i)
                    if i + 2 < TT:
                        load_x(e, i + 2)

            pool.wait_ge(ada_used, NM * KT)
            post_dmas(2)
            post_dmas(3)
            pool.wait_ge(c_lo_r, 2 * CT)
            for e in range(4, 8):
                post_dmas(e)
            for i in range(TT):
                pool.wait_ge(x1_stored[i], 16 * 6)

        @block.scalar
        def _(act):
            one = Chain(act, act_self)

            def split_hi(dst, src, s):
                nc.scalar.activation(dst, src, ACT.Copy).then_inc(s, 1)

            def post_stats(e):
                ys = post_y(e)
                if e >= 3:
                    act.wait_ge(x1_ready, 4 * (e - 2))
                for i in range(TT):
                    if e in (4, 5):
                        act.wait_ge(step_act, step_reads(OUT0 + NOUT * (e % 2) + NB_D * (i + 1) - 1)[1])
                    else:
                        G = LAST if e < 4 else G2 + LAST
                        act.wait_ge(y_done, 16 * G + 8 * (e % 2) + NB_D * (i + 1))
                    one(nc.scalar.activation(junk(e), ys[i], ACT.Square, accum_out=stat[:, SSQ, i:i + 1]))
                nc.scalar.activation(stat[:, ROOT, :], stat[:, SSQ, :], ACT.Sqrt, bias=eps_col[:, 0:1],
                                     scale=1.0 / D).then_inc(root_y, 1)

            def pre_stats(e):
                xs = pre_x(e)
                if e < 2:
                    act.wait_ge((x0_in, x0b_in)[e], 16 * TT)
                    if e:
                        act.wait_ge(rstd_x, 1)
                for i in range(TT):
                    if e >= 2:
                        act.wait_ge(x1_ready, 4 * (e - 2) + i + 1)
                    one(nc.scalar.activation(junk(e), xs[i], ACT.Square, accum_out=stat[:, SSQ, i:i + 1]))
                nc.scalar.activation(stat[:, ROOT, :], stat[:, SSQ, :], ACT.Sqrt, bias=eps_col[:, 0:1],
                                     scale=1.0 / D).then_inc(root_x, 1)

            def pre_xhat(e):
                xs = pre_x(e)
                act.wait_ge(rstd_x, e + 1)
                for i in range(TT):
                    if e >= 2:
                        act.wait_ge(x1_stored[i], 16 * (e - 1))
                    nc.scalar.activation(xs[i], xs[i], ACT.Copy, scale=stat[:, RSTDX, i:i + 1]).then_inc(xhat_r, 1)

            def h_unit(e, j):
                s, H = e // 2, e % 2
                n = 8 * e + j
                act.wait_ge(t_mm, n + 1)
                if n == 0:
                    act.wait_ge(amul_ready, 1)
                if n >= 2:
                    act.wait_ge(h_lo_r, n - 1)
                nc.scalar.activation(hf[n % 2], bank[t_bank(e, j)][:, :], ACT.Identity,
                                     bias=modcol[:, 3 * s, j:j + 1], scale=amul[:, s, j:j + 1]).then_inc(hf_done, 1)
                act.wait_ge(hf_done, n + 1)
                nc.scalar.activation(h_hi[:, j, H * HT:(H + 1) * HT], hf[n % 2], ACT.Copy).then_inc(h_hi_r, 1)

            def gateb(s):
                act.wait_ge(gb_mm, s + 1)
                if s:
                    act.wait_ge(x1_ready, (0, 8, 16)[s])
                for d in range(NB_D):
                    nc.scalar.activation(gate_b[:, d * 512:(d + 1) * 512], bank[4 + d][:, :], ACT.Copy).then_inc(gb_done, 1)

            def split_gu(s, G, f):
                for which in range(2):
                    act.wait_ge((raw0_in, raw1_in)[which], 16 * (2 * G + 1) if which == 0 else 16 * (G + 1))
                src = raw[:, :, :].rearrange("p (w a) b -> p w (a b)", w=2).rearrange("p w (k f) -> p w k f", k=KT)
                for which in range(2):
                    dst = gu_hi[:, 2 * f + which, :].rearrange("p (k f) -> p k f", k=KT)
                    split_hi(dst, src[:, which, :, f * P:(f + 1) * P], gu_hi_r)

            def split_dn(G):
                act.wait_ge(raw0_in, 16 * (2 * G + 2))
                split_hi(dn_hi[:, :, :], raw[:, 0:FG, :], dn_hi_r)

            def unit(G, h, f, used):
                n = 4 * G + 2 * h + f
                act.wait_ge(gate_mm, n + 1)
                if not (isinstance(n, int) and n == 0):
                    act.wait_ge(gate_free, n)
                nc.scalar.activation(th[:, :], bank[f][:, :], ACT.Tanh, scale=0.5).then_inc(th_done, 1)
                act.wait_ge(up_free, n + 1)
                if used:
                    act.wait_ge(down_mm, 16 * (G - 1) + 8 * h + 8)
                nc.scalar.activation(act_hi[:, h, f * HT:(f + 1) * HT], a_full[:, :], ACT.Copy).then_inc(act_hi_r, 1)

            def middle(s, G):
                act.wait_ge(up_mm, 4 * G)
                split_gu(s, G, 1)
                unit(G, 0, 0, True)
                unit(G, 0, 1, True)
                act.wait_ge(down_mm, 16 * G)
                split_dn(G)
                unit(G, 1, 0, True)
                act.wait_ge(up_mm, 4 * G + 3)
                split_gu(s, G + 1, 0)
                unit(G, 1, 1, True)

            def ffn(s, G0):
                eB = 4 * s + 1
                if s:
                    act.wait_ge(step_mm, OUT0 + 2 * NOUT)
                split_gu(s, G0, 0)
                split_gu(s, G0, 1)
                split_dn(G0)
                if s == 0:
                    pre_stats(1)
                    pre_xhat(1)
                else:
                    post_stats(eB)
                    pre_stats(eB)
                    pre_xhat(eB)
                unit(G0, 0, 0, False)
                unit(G0, 0, 1, False)
                for j in range(KT):
                    h_unit(eB, j)
                unit(G0, 1, 0, False)
                act.wait_ge(up_mm, 4 * G0 + 3)
                split_gu(s, G0 + 1, 0)
                unit(G0, 1, 1, False)
                with act.Fori(G0 + 1, G0 + LAST) as G:
                    middle(s, G)
                G = G0 + LAST
                act.wait_ge(up_mm, 4 * G)
                split_gu(s, G, 1)
                unit(G, 0, 0, True)
                gateb(0 if s == 0 else 2)
                act.wait_ge(down_mm, 16 * G)
                split_dn(G)
                unit(G, 0, 1, True)
                eA = 4 * s + 2
                post_stats(eA)
                unit(G, 1, 0, True)
                if s == 0:
                    pre_stats(eA)
                    pre_xhat(eA)
                unit(G, 1, 1, True)
                if s == 0:
                    for n in range(4):
                        ring_split(n)
                    for j in range(KT):
                        h_unit(eA, j)
                else:
                    post_stats(eA + 1)

            def ring_split(n):
                kind, i = RING[n]
                act.wait_ge(ring_in[n % 4], RING_COUNT[n])
                if kind == "in" and i < 4:
                    act.wait_ge(up_mm, 4 * LAST + 3 + i // 2)
                elif kind == "in":
                    act.wait_ge(step_mm, i - 3)
                elif i >= 4:
                    act.wait_ge(down_mm, 16 * NG)
                else:
                    act.wait_ge(step_mm, 2 * NIN - 3 + i)
                split_hi(ring_dst(n)[0], raw[:, n % 4, :], ring_hi)

            act.wait_ge(vec_ready, 1)
            nc.scalar.activation(silu_c[:, :], c_col, ACT.Tanh, scale=0.5).then_inc(thc_done, 1)
            act.wait_ge(const_ready, 3)
            pre_stats(0)
            pre_xhat(0)
            for j in range(KT):
                h_unit(0, j)
            ffn(0, 0)

            def step_read(st):
                act.wait_ge(step_mm, st + 1)
                b = bank[st % 3]
                if st >= OUT0:
                    u = st - OUT0
                    t, d = u // NB_D, u % NB_D
                    y = post_y(4 + t // TT)[t % TT]
                    if st == OUT0:
                        act.wait_ge(ring_lo, len(RING))
                    nc.scalar.activation(y[:, d * 512:(d + 1) * 512], b[:, :], ACT.Copy).then_inc(step_act, 1)
                    return
                half, (t, j) = st // NIN, TILES[st % NIN]
                if t == "b":
                    n = half * CT + j
                    if n:
                        act.wait_ge(step_dve, n)
                    nc.scalar.activation(th[:, :], b[:, :], ACT.Tanh, scale=0.5).then_inc(step_act, 1)
                elif t == "k":
                    nc.scalar.activation(k_buf[:, half * HT:(half + 1) * HT], b[:, :], ACT.Copy).then_inc(step_act, 1)
                elif t == "v":
                    nc.scalar.activation(a_full[:, :], b[:, :], ACT.Copy).then_inc(step_act, 1)
                elif t == "q":
                    nc.scalar.activation(q_buf[:, :, j, :], b[:, :].rearrange("p (n t) -> p n t", t=CH), ACT.Copy, scale=float(HD) ** -0.5).then_inc(step_act, 1)

            def v_rows(half):
                act.wait_ge(vt_mm, half + 1)
                vb = bank[3][:, :].rearrange("p (t d) -> p t d", t=TT)
                if half:
                    act.wait_ge(o_mm, 8)
                    nc.scalar.activation(v_even[64:128, 0, :], v_odd[64:128, TT - 1, :], ACT.Copy).then_inc(act_self, 1)
                    one.n += 1
                    act.wait_ge(act_self, one.n)
                nc.scalar.activation(v_odd[:, :, :], vb, ACT.Copy)
                nc.scalar.activation(v_even[0:64, :, :], vb[0:64, :, :], ACT.Copy)
                nc.scalar.activation(v_even[64:128, 1:TT, :], vb[64:128, 0:TT - 1, :], ACT.Copy).then_inc(vt_done, 1)

            def layer_norm(half):
                for ct in range(CT):
                    n = half * CT + ct
                    act.wait_ge(cen_done, n + 1)
                    if n >= 2:
                        act.wait_ge(var_mm, n - 1)
                    nc.scalar.activation(xring[:, n % 2, 0:512], acc[:, ct, :], ACT.Square).then_inc(sq_done, 1)
                act.wait_ge(var_mm, CT * (half + 1))
                one(nc.scalar.activation(stat[:, ROOT, :], bank[3][:, 0:TT], ACT.Sqrt, bias=eps_col[:, 0:1],
                                         scale=1.0 / CONV))
                nc.scalar.activation(stat[:, VAR, :], bank[3][:, 0:TT], ACT.Identity, bias=eps_col[:, 0:1],
                                     scale=1.0 / CONV).then_inc(lroot, 1)
                for ct in range(CT):
                    n = half * CT + ct
                    act.wait_ge(yn_done, n + 1)
                    one(nc.scalar.activation(xring[:, 0, 512:1024], acc[:, ct, :], ACT.Identity,
                                             bias=lnb_col[:, ct:ct + 1], scale=lng_col[:, ct:ct + 1]))
                    if n:
                        act.wait_ge(c_lo_r, n)
                    nc.scalar.activation(xring[:, 1, 512:1024], xring[:, 0, 512:1024], ACT.Tanh).then_inc(lth_done, 1)
                    act.wait_ge(lf_done, n + 1)
                    nc.scalar.activation(h_hi[:, ct, half * HT:(half + 1) * HT], xring[:, 1, 512:1024],
                                         ACT.Copy).then_inc(c_hi_r, 1)

            def attention(st):
                ns, nt, no = slots(st)
                if no is not None:
                    act.wait_ge(o_mm, no + 1)
                    nc.scalar.activation(h_hi[:, 4:8, no * CH:(no + 1) * CH],
                                         bank[7][:, 0:QT * CH].rearrange("p (g t) -> p g t", g=QT),
                                         ACT.Copy).then_inc(o_hi_r, 1)
                if nt is not None:
                    act.wait_ge(pT_mm, nt + 1)
                    if nt:
                        act.wait_ge(o_mm, nt)
                    nc.scalar.activation(pT[:, :], bank[6][:, :], ACT.Copy).then_inc(pT_r, 1)
                if ns is not None:
                    act.wait_ge(mx_r, ns + 1)
                    s = s01[:, ns % 2, :].rearrange("p (i k) -> p i k", i=4)
                    for i in range(4):
                        nc.scalar.activation(s[:, i, :], s[:, i, :], ACT.Exp, bias=stat[:, NEGM, i:i + 1],
                                             accum_out=stat[:, SUMS, i:i + 1])
                    nc.scalar.activation(stat[:, ES, :], stat[:, DIFF, :], ACT.Exp).then_inc(p_r, 1)

            done = 4
            for st in range(OUT0 + 2 * NOUT):
                while done < ring_upto(st):
                    ring_split(done)
                    done += 1
                step_read(st)
                if st == NORM_B[0]:
                    post_stats(3)
                if st == NORM_B[1]:
                    pre_stats(3)
                if st == NORM_B[2]:
                    pre_xhat(3)
                if st in TB_STEPS:
                    for j in range(2):
                        h_unit(3, 2 * (st - TB_STEPS[0]) + j)
                if st == GATEB_STEP:
                    gateb(1)
                if st < OUT0 and st % NIN == VT_STEP:
                    v_rows(st // NIN)
                attention(st)
                if st in LN_STEP:
                    layer_norm(LN_STEP.index(st))
                if st == OUT0 + NOUT:
                    post_stats(4)
                if st == OUT0 + NOUT + 2:
                    pre_stats(4)
                    pre_xhat(4)
                if st in TA_STEPS:
                    for j in range(2):
                        h_unit(4, 2 * (st - TA_STEPS[0]) + j)
            ffn(1, G2)

        @block.vector
        def _(dve):
            one = Chain(dve, dve_self)
            TTo, TS, STT = nc.vector.tensor_tensor, nc.vector.tensor_scalar, nc.vector.scalar_tensor_tensor

            def f32(ap):
                return ap.bitcast(F32)

            def rstd(dst, var_src, n_inv):
                if n_inv is not None:
                    one(TS(stat[:, VAR, :], var_src, n_inv, EPS, ALU.mult, ALU.add))
                one(nc.vector.reciprocal(stat[:, T1, :], stat[:, ROOT, :]))
                one(TTo(stat[:, T2, :], stat[:, T1, :], stat[:, T1, :], ALU.mult))
                one(TTo(stat[:, T2, :], stat[:, T2, :], stat[:, VAR, :], ALU.mult))
                one(TS(stat[:, T2, :], stat[:, T2, :], -0.5, 1.5, ALU.mult, ALU.add))
                return TTo(dst, stat[:, T1, :], stat[:, T2, :], ALU.mult)

            def post(e, part):
                ys = post_y(e)
                if part == 0:
                    dve.wait_ge(root_y, e - 1)
                    one(rstd(stat[:, RSTDY, :], stat[:, SSQ, :], 1.0 / D))
                    dve.wait_ge(gb_done, NB_D * ((e - 2) // 2 + 1))
                for i in (0, 1) if part == 0 else (2, 3):
                    n = 4 * (e - 2) + i
                    one(STT(ys[i], ys[i], stat[:, RSTDY, i:i + 1], gate_b[:, :], ALU.mult, ALU.mult))
                    dve.wait_ge(x_tile_in[n % 2], 16 * (n // 2 + 1))
                    TTo(ys[i], ys[i], xring[:, n % 2, :], ALU.add).then_inc(x1_ready, 1)

            def pre_rstd(e):
                dve.wait_ge(root_x, e + 1)
                rstd(stat[:, RSTDX, :], stat[:, SSQ, :], 1.0 / D).then_inc(rstd_x, 1)

            def h_unit(e, j):
                n, H = 8 * e + j, e % 2
                dve.wait_ge(h_hi_r, n + 1)
                cols = slice(H * HT, (H + 1) * HT)
                TTo(h_lo[:, j, cols], hf[n % 2], f32(h_hi[:, j, cols]), ALU.subtract).then_inc(h_lo_r, 1)

            def gateb(s):
                if s:
                    dve.wait_ge(gb_mm, s)
                if s == 2:
                    dve.wait_ge(pn_r, NCH)
                for j in range(KT):
                    ins = TS(diag[:, j * P:(j + 1) * P], ident[:, :], gcol[:, s, j:j + 1], None, ALU.mult)
                ins.then_inc(diag_r, 1)

            def mods(s):
                one(STT(amul[:, s, :], modcol[:, 3 * s + 1, :], 1.0, npre_col[:, s, :], ALU.add, ALU.mult))

            def mod_gate(s):
                one(STT(gcol[:, s, :], modcol[:, 3 * s + 2, :], RES[s], npost_col[:, s, :], ALU.mult, ALU.mult))

            def ada_rows(m, kts, slot_of, count_of):
                for kt in kts:
                    sl, cnt = slot_of(kt), count_of(kt)
                    dve.wait_ge(ada_in[sl], cnt)
                    src = raw[:, sl, :] if sl < 4 else xring[:, sl - 4, :]
                    if kt == 0:
                        TS(ada_acc, src, silu_c[:, 0:1], None, ALU.mult).then_inc(ada_used, 1)
                    else:
                        dve.wait_ge(ada_used, m * KT + kt)
                        STT(ada_acc, src, silu_c[:, kt:kt + 1], ada_acc, ALU.mult, ALU.add).then_inc(ada_used, 1)

            def ada_vec(m):
                dve.wait_ge(ada_mm, m + 1)
                mc = modcol[:, m, :] if isinstance(m, int) else modcol[:, bass.ds(m, 1), :]
                bc = ada_b_col[:, m, :] if isinstance(m, int) else ada_b_col[:, bass.ds(m, 1), :]
                src = bank[4][:, 0:KT] if isinstance(m, int) else bank[4][:, 0:KT].rearrange("p (a k) -> p a k", a=1)
                TTo(mc, src, bc, ALU.add).then_inc(ada_col, 1)

            def split_gu(G, f):
                src = raw[:, :, :].rearrange("p (w a) b -> p w (a b)", w=2).rearrange("p w (k f) -> p w k f", k=KT)
                for which in range(2):
                    dve.wait_ge(gu_hi_r, 4 * G + 2 * f + which + 1)
                    hi = gu_hi[:, 2 * f + which, :].rearrange("p (k f) -> p k f", k=KT)
                    lo = gu_lo[:, 2 * f + which, :].rearrange("p (k f) -> p k f", k=KT)
                    TTo(lo, src[:, which, :, f * P:(f + 1) * P], f32(hi), ALU.subtract).then_inc(gu_lo_r, 1)

            def split_dn(G):
                dve.wait_ge(dn_hi_r, G + 1)
                TTo(dn_lo[:, :, :], raw[:, 0:FG, :], f32(dn_hi[:, :, :]), ALU.subtract).then_inc(dn_lo_r, 1)

            def unit(G, h, f):
                n = 4 * G + 2 * h + f
                dve.wait_ge(th_done, n + 1)
                if not (isinstance(n, int) and n == 0):
                    dve.wait_ge(act_lo_r, n)
                STT(a_full[:, :], th[:, :], 1.0, bank[f][:, :], ALU.add, ALU.mult).then_inc(gate_free, 1)
                dve.wait_ge(up_mm, n + 1)
                dve.wait_ge(gate_free, n + 1)
                STT(a_full[:, :], a_full[:, :], 0.5, bank[2 + f][:, :], ALU.mult, ALU.mult).then_inc(up_free, 1)
                dve.wait_ge(act_hi_r, n + 1)
                cols = slice(f * HT, (f + 1) * HT)
                TTo(act_lo[:, h, cols], a_full[:, :], f32(act_hi[:, h, cols]), ALU.subtract).then_inc(act_lo_r, 1)

            def add_y(G, h, i, first):
                m = 16 * G + 8 * h + i
                t, d = TT * h + i // NB_D, i % NB_D
                y = y_ffn[:, t, d * 512:(d + 1) * 512]
                dve.wait_ge(down_mm, m + 1)
                if first:
                    if h == 0 and i == 0 and isinstance(m, int) and m:
                        pass
                    nc.vector.tensor_copy(y, bank[4 + i % 4][:, :]).then_inc(y_done, 1)
                else:
                    dve.wait_ge(y_done, m - 15)
                    TTo(y, bank[4 + i % 4][:, :], y, ALU.add).then_inc(y_done, 1)

            def middle(G, ada_m, prev_first):
                split_gu(G, 1)
                unit(G, 0, 0)
                if ada_m is not None:
                    sl = lambda kt: 4 + kt % 2
                    cnt = lambda kt: 16 * (4 * (ada_m - 2) + 2 + kt // 2 + 1)
                    ada_rows(ada_m, range(0, 4), sl, cnt)
                unit(G, 0, 1)
                if ada_m is not None:
                    ada_rows(ada_m, range(4, 8), sl, cnt)
                for i in range(8):
                    add_y(G - 1, 1, i, prev_first)
                split_dn(G)
                if ada_m is not None:
                    ada_vec(ada_m)
                unit(G, 1, 0)
                for i in range(8):
                    add_y(G, 0, i, False)
                split_gu(G + 1, 0)
                unit(G, 1, 1)

            def ffn(s, G0):
                eB = 4 * s + 1
                split_gu(G0, 0)
                split_gu(G0, 1)
                split_dn(G0)
                if s == 0:
                    pre_rstd(1)
                else:
                    post(eB, 0)
                    post(eB, 1)
                    pre_rstd(eB)
                unit(G0, 0, 0)
                unit(G0, 0, 1)
                for i in range(8):
                    if s == 0 or True:
                        add_y(G0, 0, i, True)
                for j in range(KT):
                    h_unit(eB, j)
                unit(G0, 1, 0)
                split_gu(G0 + 1, 0)
                unit(G0, 1, 1)
                if s == 0:
                    middle(1, 2, True)
                    with dve.Fori(2, NM - 1) as G:
                        middle(G, G + 1, False)
                    with dve.Fori(NM - 1, LAST) as G:
                        middle(G, None, False)
                else:
                    middle(G0 + 1, None, True)
                    with dve.Fori(G0 + 2, G0 + LAST) as G:
                        middle(G, None, False)
                G = G0 + LAST
                if s == 0:
                    dve.wait_ge(ada_col, NM)
                    for k in (1, 2):
                        mods(k)
                    for k in range(3):
                        mod_gate(k)
                split_gu(G, 1)
                gateb(0 if s == 0 else 2)
                unit(G, 0, 0)
                for i in range(8):
                    add_y(G - 1, 1, i, False)
                split_dn(G)
                unit(G, 0, 1)
                for i in range(8):
                    add_y(G, 0, i, False)
                eA = 4 * s + 2
                post(eA, 0)
                unit(G, 1, 0)
                post(eA, 1)
                if s == 0:
                    pre_rstd(eA)
                unit(G, 1, 1)
                if s == 0:
                    for n in range(4):
                        ring_split(n)
                    for j in range(KT):
                        h_unit(eA, j)
                        add_y(G, 1, j, False)
                else:
                    for i in range(8):
                        add_y(G, 1, i, False)
                    post(eA + 1, 0)
                    post(eA + 1, 1)

            def ring_split(n):
                dve.wait_ge(ring_hi, n + 1)
                hi, lo = ring_dst(n)
                TTo(lo, raw[:, n % 4, :], f32(hi), ALU.subtract).then_inc(ring_lo, 1)

            dve.wait_ge(vec_mm, 1)
            for at, n in ((0, 120), (P, TAPS * CT), (2 * P, 20)):
                last = nc.vector.tensor_copy(vecs[:, at:at + n], bank[4][:, at:at + n])
            last.then_inc(vec_ready, 1)
            dve.wait_ge(vec_ready, 1)
            one(TS(lng_col, lng_col, 0.5, None, ALU.mult))
            one(TS(lnb_col, lnb_col, 0.5, None, ALU.mult))
            one(TS(taps_col, taps_col, 0.5, None, ALU.mult))
            dve.wait_ge(const_ready, 2)
            dist = s01[:, 0, 0:P]
            one(STT(dist, dist, -1.0, dist, ALU.mult, ALU.max))
            for i in range(4):
                for hh in range(2):
                    rows = slice(64 * hh, 64 * hh + 64)
                    slope = 2.0 ** (-8.0 * (2 * i + hh + 1) / NH)
                    TS(alibi[rows, 0, i, :], dist[rows, :], -slope, None, ALU.mult)
                    TS(alibi[rows, 1, i, 0:CH], dist[rows, CH:P], -slope, None, ALU.mult)
                    last = TS(alibi[rows, 1, i, CH:P], dist[rows, 0:CH], -slope, None, ALU.mult)
            last.then_inc(const_ready, 1)
            dve.wait_ge(thc_done, 1)
            one(STT(silu_c[:, :], silu_c[:, :], 1.0, c_col, ALU.add, ALU.mult))
            one(TS(silu_c[:, :], silu_c[:, :], 0.5, None, ALU.mult))
            dve.wait_ge(const_ready, 3)
            dve.wait_ge(vec_in, 16 * 10)
            for m in range(2):
                ada_rows(m, range(KT), lambda kt: (m * KT + kt) % 6, lambda kt: 16 * ((m * KT + kt) // 6 + 1))
                ada_vec(m)
                dve.wait_ge(ada_col, m + 1)
            pre_rstd(0)
            STT(amul[:, 0, :], modcol[:, 1, :], 1.0, npre_col[:, 0, :], ALU.add, ALU.mult).then_inc(amul_ready, 1)
            for j in range(KT):
                h_unit(0, j)
            ffn(0, 0)

            def glu(half, ct):
                n = half * CT + ct
                st = half * NIN + 2 * ct + 1
                if half == 0:
                    nc.vector.memset(u_buf[:, ct, 0:HIST], 0.0)
                else:
                    one(nc.vector.tensor_copy(u_buf[:, ct, 0:HIST], u_buf[:, ct, HT:HT + HIST]))
                dve.wait_ge(step_act, step_reads(st - 1)[1])
                dve.wait_ge(step_mm, st + 1)
                STT(u_buf[:, ct, HIST:HIST + HT], th[:, :], 1.0, bank[st % 3][:, :], ALU.add,
                    ALU.mult).then_inc(step_dve, 1)
                dve.wait_ge(step_dve, n + 1)

            def conv(half, ct, first, end):
                if half and ct == 0 and first == 0:
                    dve.wait_ge(c_hi_r, CT)
                for tap in range(first, end):
                    src = u_buf[:, ct, tap:tap + HT]
                    w = taps_col[:, tap, ct:ct + 1]
                    if tap == 0:
                        ins = TS(acc[:, ct, :], src, w, convb_col[:, ct:ct + 1], ALU.mult, ALU.add)
                    else:
                        ins = STT(acc[:, ct, :], src, w, acc[:, ct, :], ALU.mult, ALU.add)
                    if ct == CT - 1 and tap == TAPS - 1:
                        ins.then_inc(conv_done, 1)
                        dve.wait_ge(conv_done, 2 + half)
                    else:
                        one(ins)

            def layer_norm(half):
                dve.wait_ge(mean_mm, half + 1)
                for ct in range(CT):
                    STT(acc[:, ct, :], bank[3][:, :], -1.0 / CONV, acc[:, ct, :], ALU.mult, ALU.add).then_inc(cen_done, 1)
                dve.wait_ge(lroot, half + 1)
                one(rstd(stat[:, RSTDY, :], None, None))
                for i in range(TT):
                    ins = TS(a_full[:, i * P:(i + 1) * P], ident[:, :], stat[:, RSTDY, i:i + 1], None, ALU.mult)
                ins.then_inc(ldiag, 1)
                dve.wait_ge(lb_mm, half + 1)
                for ct in range(CT):
                    TTo(acc[:, ct, :], bank[3][:, :], acc[:, ct, :], ALU.mult).then_inc(yn_done, 1)
                for ct in range(CT):
                    n = half * CT + ct
                    dve.wait_ge(lth_done, n + 1)
                    z, t = xring[:, 0, 512:1024], xring[:, 1, 512:1024]
                    STT(t, t, 1.0, z, ALU.add, ALU.mult).then_inc(lf_done, 1)
                    dve.wait_ge(c_hi_r, n + 1)
                    cols = slice(half * HT, (half + 1) * HT)
                    TTo(h_lo[:, ct, cols], t, f32(h_hi[:, ct, cols]), ALU.subtract).then_inc(c_lo_r, 1)

            def attention(st):
                ns, nt, no = slots(st)
                if no is not None:
                    dve.wait_ge(o_hi_r, no + 1)
                    cols = slice(no * CH, (no + 1) * CH)
                    TTo(h_lo[:, 4:8, cols], bank[7][:, 0:QT * CH].rearrange("p (g t) -> p g t", g=QT),
                        f32(h_hi[:, 4:8, cols]), ALU.subtract).then_inc(o_lo_r, 1)
                if ns is not None:
                    s = s01[:, ns % 2, :].rearrange("p (i k) -> p i k", i=4)
                    tab = alibi[:, 1 - ns % 2, :, :]
                    if ns >= 2:
                        dve.wait_ge(pT_mm, ns - 1)
                    dve.wait_ge(s_mm, ns + 1)
                    keys = slice(0, CH if ns == 0 else P)
                    if ns == 0:
                        dve.wait_ge(gb_mm, 2)
                        one(nc.vector.memset(s[:, :, CH:P], NEG))
                    for kv in range(2):
                        sc = bank[4 + kv][:, 0:2 * P].rearrange("p (i k) -> p i k", i=2)
                        ins = TTo(s[:, 2 * kv:2 * kv + 2, keys], sc[:, :, keys], tab[:, 2 * kv:2 * kv + 2, keys], ALU.add)
                        if kv:
                            ins.then_inc(s_read, 1)
                        else:
                            one.mark(ins)
                    dve.wait_ge(dve_self, one.n)
                    dve.wait_ge(s_read, ns + 1)
                    one(nc.vector.tensor_reduce(stat[:, MX, :], s, AX.X, ALU.max))
                    one(TTo(stat[:, MX, :], stat[:, MX, :], sink_col[:, :], ALU.max))
                    TS(stat[:, NEGM, :], stat[:, MX, :], -1.0, None, ALU.mult)
                    TTo(stat[:, DIFF, :], sink_col[:, :], stat[:, MX, :], ALU.subtract).then_inc(mx_r, 1)
                    dve.wait_ge(p_r, ns + 1)
                    one(TTo(stat[:, DEN, :], stat[:, SUMS, :], stat[:, ES, :], ALU.add))
                    one(nc.vector.reciprocal(stat[:, RDEN, :], stat[:, DEN, :]))
                    for i in range(4):
                        ins = TS(s[:, i, :], s[:, i, :], stat[:, RDEN, i:i + 1], None, ALU.mult)
                    ins.then_inc(pn_r, 1)

            nc_done = 4
            for st in range(OUT0 + 2 * NOUT):
                while nc_done < ring_upto(st):
                    ring_split(nc_done)
                    nc_done += 1
                if st < OUT0 and TILES[st % NIN][0] == "a":
                    glu(st // NIN, TILES[st % NIN][1])
                if st == NORM_B[0]:
                    post(3, 0)
                if st == NORM_B[1]:
                    post(3, 1)
                    pre_rstd(3)
                if st in TB_STEPS:
                    for j in range(2):
                        h_unit(3, 2 * (st - TB_STEPS[0]) + j)
                if st == GATEB_STEP:
                    gateb(1)
                if st == VT_STEP:
                    dve.wait_ge(h_lo_r, 32)
                    nc.vector.memset(v_even[64:128, 0, :], 0.0).then_inc(conv_done, 1)
                for a in CONV_AT.get(st, []):
                    conv(*a)
                attention(st)
                if st in LN_STEP:
                    layer_norm(LN_STEP.index(st))
                if st == OUT0 + NOUT:
                    post(4, 0)
                if st == OUT0 + NOUT + 1:
                    post(4, 1)
                if st == OUT0 + NOUT + 2:
                    pre_rstd(4)
                if st in TA_STEPS:
                    for j in range(2):
                        h_unit(4, 2 * (st - TA_STEPS[0]) + j)
            ffn(1, G2)

        @block.tensor
        def _(pe):
            mm = nc.tensor.matmul

            def split_mm(dst, lhs, rhs, first, last):
                mm(dst, lhs[0], rhs[0], start=first, stop=False)
                mm(dst, lhs[0], rhs[1], start=False, stop=False)
                return mm(dst, lhs[1], rhs[0], start=False, stop=last)

            def h_cols(kt, H):
                cols = slice(H * HT, (H + 1) * HT)
                return h_hi[:, kt, cols], h_lo[:, kt, cols]

            def t_unit(e, j):
                n = 8 * e + j
                if j == 0:
                    pe.wait_ge(xhat_r, TT * (e + 1))
                t_free(e, j)
                b = bank[t_bank(e, j)]
                xs = pre_x(e)
                for i in range(TT):
                    last = nc.tensor.transpose(b[:, i * P:(i + 1) * P], xs[i][:, j * P:(j + 1) * P], ident[:, :])
                last.then_inc(t_mm, 1)

            def t_free(e, j):
                n = 8 * e + j
                if j >= 4:
                    pe.wait_ge(hf_done, n - 3)
                elif e == 0:
                    pe.wait_ge(ada_col, 2)
                elif e == 1:
                    pe.wait_ge(hf_done, 8)
                    pe.wait_ge(y_done, 8)
                elif e == 2:
                    pe.wait_ge(up_free, 4 * NG)
                elif e == 3:
                    pe.wait_ge(y_done, 16 * NG)
                elif e == 4:
                    pe.wait_ge(o_lo_r, NCH)
                else:
                    pe.wait_ge(hf_done, 8 * 5)
                    pe.wait_ge(y_done, 16 * G2 + 8)

            def gate_up(G, h, f, s):
                n = 4 * G + 2 * h + f
                if h == 0:
                    pe.wait_ge(gu_lo_r, 4 * G + 2 * (f + 1))
                for which in range(2):
                    if not (isinstance(n, int) and n < 2):
                        pe.wait_ge((gate_free, up_free)[which], n - 1)
                    w = gu_hi[:, 2 * f + which, :], gu_lo[:, 2 * f + which, :]
                    for kt in range(KT):
                        k = slice(kt * P, (kt + 1) * P)
                        last = split_mm(bank[2 * which + f][:, :], (w[0][:, k], w[1][:, k]), h_cols(kt, h),
                                        kt == 0, kt == KT - 1)
                    last.then_inc((gate_mm, up_mm)[which], 1)

            def down(G, h, i):
                m = 16 * G + 8 * h + i
                if i == 0:
                    pe.wait_ge(act_lo_r, 4 * G + 2 * h + 2)
                    pe.wait_ge(dn_lo_r, G + 1)
                if not (isinstance(m, int) and m < 4):
                    pe.wait_ge(y_done, m - 3)
                t, d = i // NB_D, i % NB_D
                for f in range(FG):
                    a = slice(f * HT + t * P, f * HT + (t + 1) * P)
                    n = slice(d * 512, (d + 1) * 512)
                    last = split_mm(bank[4 + i % 4][:, :], (act_hi[:, h, a], act_lo[:, h, a]),
                                    (dn_hi[:, f, n], dn_lo[:, f, n]), f == 0, f == FG - 1)
                last.then_inc(down_mm, 1)

            def ada_reduce(m):
                pe.wait_ge(ada_used, (m + 1) * KT)
                for j in range(KT):
                    last = mm(bank[4][:, j:j + 1], ada_acc[:, j * P:(j + 1) * P], ones[:, 0:1], start=True, stop=True)
                last.then_inc(ada_mm, 1)

            def gateb(s):
                pe.wait_ge(diag_r, s + 1)
                for j in range(KT):
                    last = mm(bank[4 + j // 4][:, (j % 4) * P:(j % 4 + 1) * P], ones[:, :],
                              diag[:, j * P:(j + 1) * P], start=True, stop=True)
                last.then_inc(gb_mm, 1)

            def middle(G, s, ada_m):
                gate_up(G, 0, 0, s)
                gate_up(G, 0, 1, s)
                for i in range(8):
                    down(G - 1, 1, i)
                if ada_m is not None:
                    pe.wait_ge(y_done, 16 * G - 3)
                    ada_reduce(ada_m)
                gate_up(G, 1, 0, s)
                if ada_m is not None:
                    pe.wait_ge(ada_col, ada_m + 1)
                for i in range(8):
                    down(G, 0, i)
                gate_up(G, 1, 1, s)

            def ffn(s, G0):
                eB = 4 * s + 1
                pe.wait_ge(h_lo_r, 8 * eB)
                if s:
                    pe.wait_ge(step_act, step_reads(OUT0 + 2 * NOUT - 1)[1])
                gate_up(G0, 0, 0, s)
                gate_up(G0, 0, 1, s)
                if s:
                    pe.wait_ge(hf_done, 8 * 5)
                for i in range(8):
                    down(G0, 0, i)
                for j in range(KT):
                    t_unit(eB, j)
                pe.wait_ge(h_lo_r, 8 * (eB + 1))
                gate_up(G0, 1, 0, s)
                gate_up(G0, 1, 1, s)
                if s == 0:
                    with pe.Fori(1, NM - 1) as G:
                        middle(G, 0, G + 1)
                    with pe.Fori(NM - 1, LAST) as G:
                        middle(G, 0, None)
                else:
                    with pe.Fori(G0 + 1, G0 + LAST) as G:
                        middle(G, 1, None)
                G = G0 + LAST
                gate_up(G, 0, 0, s)
                for i in range(8):
                    down(G - 1, 1, i)
                pe.wait_ge(y_done, 16 * G - 2)
                gateb(0 if s == 0 else 2)
                gate_up(G, 0, 1, s)
                pe.wait_ge(gb_done, 2 if s == 0 else 6)
                for i in range(8):
                    down(G, 0, i)
                gate_up(G, 1, 0, s)
                gate_up(G, 1, 1, s)
                for i in range(4):
                    down(G, 1, i)
                if s == 0:
                    for j in range(4):
                        t_unit(2, j)
                for i in range(4, 8):
                    if s == 0:
                        t_unit(2, i)
                    down(G, 1, i)

            pe.wait_ge(vec_in, 16 * 10)
            pe.wait_ge(pool_self, 2)
            for n, rows in enumerate((120, TAPS * CT, 20)):
                last = nc.tensor.transpose(bank[4][:, n * P:n * P + rows], vec_raw[0:rows, n * P:(n + 1) * P],
                                           ident[0:rows, 0:rows])
            last.then_inc(vec_mm, 1)
            pe.wait_ge(vec_ready, 1)
            for m in range(2):
                if m:
                    pe.wait_ge(ada_col, m)
                ada_reduce(m)
            for j in range(KT):
                t_unit(0, j)
            ffn(0, 0)

            def project(st):
                half, (t, j) = st // NIN, TILES[st % NIN]
                pe.wait_ge(ring_lo, IN_AT[st] + 1)
                for kt in range(KT):
                    k = slice(kt * P, (kt + 1) * P)
                    w = gu_hi[:, st % 4, k], gu_lo[:, st % 4, k]
                    last = split_mm(bank[st % 3][:, :], w, h_cols(kt, half), kt == 0, kt == KT - 1)
                last.then_inc(step_mm, 1)

            def mix_out(st):
                u = st - OUT0
                t, d = u // NB_D, u % NB_D
                n = slice(d * 512, (d + 1) * 512)
                order = [4, 5, 6, 7, 0, 1, 2, 3]
                for k, kt in enumerate(order):
                    pe.wait_ge(ring_lo, OUT_AT[kt] + 1)
                    if kt == 4:
                        pe.wait_ge(o_lo_r, 2 * t + 2)
                    if kt == 0:
                        pe.wait_ge(c_lo_r, CT * (t // TT + 1))
                    rows = slice(t * P, (t + 1) * P)
                    w = wout_tile(kt)
                    last = split_mm(bank[st % 3][:, :], (h_hi[:, kt, rows], h_lo[:, kt, rows]),
                                    (w[0][:, n], w[1][:, n]), k == 0, k == KT - 1)
                last.then_inc(step_mm, 1)

            def v_rows(half):
                pe.wait_ge(step_act, step_reads(half * NIN + V_STEP)[1])
                if half:
                    pe.wait_ge(c_lo_r, CT * half)
                for i in range(TT):
                    last = nc.tensor.transpose(bank[3][:, i * P:(i + 1) * P], a_full[:, i * P:(i + 1) * P], ident[:, :])
                last.then_inc(vt_mm, 1)

            def attention(st):
                ns, nt, no = slots(st)
                if no is not None:
                    pe.wait_ge(pT_r, no + 1)
                    pe.wait_ge(vt_done, no // 8 + 1)
                    if no:
                        pe.wait_ge(o_lo_r, no)
                    v = v_odd[:, ((no - 1) // 2) % TT, :] if no % 2 else v_even[:, (no // 2) % TT, :]
                    for i in range(4):
                        kv, g0 = i // 2, 2 * (i % 2)
                        last = mm(bank[7][kv * HD:(kv + 1) * HD, g0 * CH:(g0 + 2) * CH],
                                  v[:, kv * HD:(kv + 1) * HD], pT[:, i * P:(i + 1) * P], start=True, stop=True)
                    last.then_inc(o_mm, 1)
                if nt is not None:
                    pe.wait_ge(pn_r, nt + 1)
                    if nt:
                        pe.wait_ge(pT_r, nt)
                    for i in range(4):
                        last = nc.tensor.transpose(bank[6][:, i * P:(i + 1) * P],
                                                   s01[:, nt % 2, i * P:(i + 1) * P], ident[:, :])
                    last.then_inc(pT_mm, 1)
                if ns is not None:
                    pe.wait_ge(step_act, step_reads((ns // 8) * NIN + NIN - 1)[1])
                    if ns:
                        pe.wait_ge(s_read, ns)
                    for i in range(4):
                        kv, g0 = i // 2, 2 * (i % 2)
                        rows = slice(kv * HD, (kv + 1) * HD)
                        q = q_buf[rows, ns % 8, g0:g0 + 2, :].rearrange("p g t -> p (g t)")
                        col = (i % 2) * P
                        if ns % 2:
                            parts = [(slice(col, col + P), slice((ns - 1) * CH, (ns + 1) * CH))]
                        else:
                            parts = [(slice(col, col + CH), slice(ns * CH, (ns + 1) * CH))]
                            if ns:
                                parts.append((slice(col + CH, col + P), slice((ns - 1) * CH, ns * CH)))
                        for to, keys in parts:
                            last = mm(bank[4 + kv][:, to], q, k_buf[rows, keys], start=True, stop=True)
                    last.then_inc(s_mm, 1)

            def layer_norm(half):
                pe.wait_ge(conv_done, 2 + half)
                pe.wait_ge(vt_done, half + 1 if half else 1)
                for ct in range(CT):
                    last = mm(bank[3][:, :], ones[:, :], acc[:, ct, :], start=ct == 0, stop=ct == CT - 1)
                last.then_inc(mean_mm, 1)
                pe.wait_ge(cen_done, CT * (half + 1))
                for ct in range(CT):
                    pe.wait_ge(sq_done, CT * half + ct + 1)
                    n = (half * CT + ct) % 2
                    for i in range(TT):
                        last = mm(bank[3][:, i:i + 1], xring[:, n, i * P:(i + 1) * P], ones[:, 0:1],
                                  start=ct == 0 and i == 0, stop=ct == CT - 1 and i == TT - 1,
                                  skip_group_check=True)
                    last.then_inc(var_mm, 1)
                pe.wait_ge(ldiag, half + 1)
                for i in range(TT):
                    last = mm(bank[3][:, i * P:(i + 1) * P], ones[:, :], a_full[:, i * P:(i + 1) * P],
                              start=True, stop=True)
                last.then_inc(lb_mm, 1)

            pe.wait_ge(h_lo_r, 8 * 3)
            for st in range(OUT0 + 2 * NOUT):
                if st >= 3:
                    pe.wait_ge(*step_reads(st - 3))
                if st == NIN:
                    pe.wait_ge(h_lo_r, 8 * 4)
                if st < OUT0:
                    project(st)
                else:
                    mix_out(st)
                if st in TB_STEPS:
                    for j in range(2):
                        t_unit(3, 2 * (st - TB_STEPS[0]) + j)
                if st == GATEB_STEP:
                    pe.wait_ge(hf_done, 8 * 4)
                    gateb(1)
                if st < OUT0 and st % NIN == VT_STEP:
                    v_rows(st // NIN)
                attention(st)
                if st in LN_STEP:
                    layer_norm(LN_STEP.index(st))
                if st in TA_STEPS:
                    for j in range(2):
                        t_unit(4, 2 * (st - TA_STEPS[0]) + j)
            ffn(1, G2)


_INS = ["x", "c", "ada_w", "ada_b", "norm_pre", "norm_post",
        "ffn1_w_gate", "ffn1_w_up", "ffn1_w_down", "ffn2_w_gate", "ffn2_w_up", "ffn2_w_down",
        "mix_w_in", "conv_w", "conv_b", "conv_ln_g", "conv_ln_b", "attn_sinks", "mix_w_out"]


def kernel(**inputs):
    import numpy as _np
    import concourse.bacc as _bacc
    from concourse import mybir as _mybir
    from concourse.bass_utils import run_bass_kernel_spmd as _run

    nc = _bacc.Bacc("TRN2", target_bir_lowering=False, num_devices=1)
    arrays, args = {}, []
    for name in _INS:
        a = _np.ascontiguousarray(inputs[name])
        arrays[f"in_{name}_dram"] = a
        args.append(nc.dram_tensor(f"in_{name}_dram", a.shape, _mybir.dt.from_np(a.dtype), kind="ExternalInput").ap())
    args.append(nc.dram_tensor("out_dram", arrays["in_x_dram"].shape, _mybir.dt.float32, kind="ExternalOutput").ap())
    layer(nc, *args)
    r = _run(nc, [arrays], core_ids=[0])
    return r.results[0]["out_dram"]
```

```python
import concourse.bass as bass
from concourse import mybir
from contextlib import ExitStack


def layer(nc, x_in, c, ada_w, ada_b, norm_pre, norm_post,
          w_gate1, w_up1, w_down1, w_gate2, w_up2, w_down2,
          w_in, conv_w, conv_b, ln_g, ln_b, sinks, w_out, out):
    F32, F32R = mybir.dt.float32, mybir.dt.float32r
    ALU, ACT, AX = mybir.AluOpType, mybir.ActivationFunctionType, mybir.AxisListType

    P = 128
    S, D = x_in.shape[1], x_in.shape[2]
    KT = D // P
    HT = S // 2
    TT = HT // P
    FF = w_down1.shape[1]
    FG = 2
    NG = FF // (FG * P)
    CONV = conv_b.shape[1]
    CT = CONV // P
    TAPS = conv_w.shape[1]
    HIST = TAPS - 1
    NH = sinks.shape[1]
    HD = 64
    CH = 64
    NCH = S // CH
    QT = NH * HD // P
    NM = 9
    NB_D = D // 512
    EPS = 1e-6
    RES = (0.5, 1.0, 0.5)
    NEG = -1e30
    LAST = NG - 1
    G2 = NG

    x_tok = x_in[0].rearrange("(t p) d -> t p d", p=P)
    out_tok = out[0].rearrange("(t p) d -> t p d", p=P)
    ffn_w = ((w_gate1[0], w_up1[0], w_down1[0]), (w_gate2[0], w_up2[0], w_down2[0]))

    ctx = ExitStack()
    with ctx:
        def sb(name, shape, dt=F32):
            return ctx.enter_context(nc.sbuf_tensor(name, shape, dt))

        def sem(name):
            return ctx.enter_context(nc.semaphore(name))

        h_hi = sb("h_hi", [P, KT, S], F32R)
        h_lo = sb("h_lo", [P, KT, S], F32R)
        yreg = sb("yreg", [P, 2 * TT * D])
        y_ffn = yreg[:, :].rearrange("p (t d) -> p t d", d=D)
        gu_hi = sb("gu_hi", [P, 4, KT * P], F32R)
        gu_lo = sb("gu_lo", [P, 4, KT * P], F32R)
        dn_hi = sb("dn_hi", [P, FG, D], F32R)
        dn_lo = sb("dn_lo", [P, FG, D], F32R)
        act_hi = sb("act_hi", [P, 2, FG * HT], F32R)
        act_lo = sb("act_lo", [P, 2, FG * HT], F32R)
        raw = sb("raw", [P, 4, KT * P])
        xring = sb("xring", [P, 2, D])
        gate_b = sb("gate_b", [P, D])
        th = sb("th", [P, HT])
        a_full = sb("a_full", [P, HT])
        s01 = sb("s01", [P, 2, 512])
        pT = sb("pT", [P, 512])
        v_even = sb("v_even", [P, TT, P])
        ident = sb("ident", [P, P])
        ones = sb("ones", [P, P])
        vecs = sb("vecs", [P, 268])
        modcol = sb("modcol", [P, NM, KT])
        amul = sb("amul", [P, 3, KT])
        gcol = sb("gcol", [P, 3, KT])
        silu_c = sb("silu_c", [P, KT])
        alibi = sb("alibi", [P, 2, 4, P])
        sink_col = sb("sink_col", [P, 4])
        eps_col = sb("eps_col", [P, 1])
        stat = sb("stat", [P, 7, 4])
        sm = sb("sm", [P, 2, 7, 4])
        lstat = sb("lstat", [P, 5, 4])
        SSQ, ROOT, VAR, T1, T2, RSTDY, RSTDX = range(7)
        MX, NEGM, DIFF, SUMS, ES, DEN, RDEN = range(7)

        o = 0
        u_buf = yreg[:, o:o + CT * (HIST + HT)].rearrange("p (c t) -> p c t", c=CT)
        o += CT * (HIST + HT)
        acc = [yreg[:, o + (ct + 1) % CT * HT:o + ((ct + 1) % CT + 1) * HT] for ct in range(CT)]
        o += CT * HT
        q_buf = yreg[:, o:o + QT * HT].rearrange("p (n g t) -> p n g t", g=QT, t=CH)
        o += QT * HT
        k_buf = yreg[:, o:o + S]
        o += S
        v_odd = yreg[:, o:o + TT * P].rearrange("p (t d) -> p t d", t=TT)
        assert o + TT * P <= 2 * TT * D

        hf = [pT[:, :], v_even[:, :, :].rearrange("p t d -> p (t d)")]
        ada_acc = s01[:, :, :].rearrange("p a b -> p (a b)")
        diag = ada_acc

        def junk(e):
            return gate_b[:, :] if e < 2 else ada_acc

        ada_start = [y_ffn[:, TT + i, :] for i in range(TT)] + [xring[:, i, :] for i in range(2)]

        swish = [(xring[:, i, 0:512], xring[:, i, 512:1024]) for i in range(2)]
        prod = [xring[:, n % 2, (n // 2) * 512:(n // 2 + 1) * 512] for n in range(4)]

        vec_raw = pT
        ada_b_col = vecs[:, 0:NM * KT].rearrange("p (m j) -> p m j", j=KT)
        npre_col = vecs[:, 72:96].rearrange("p (s j) -> p s j", j=KT)
        npost_col = vecs[:, 96:120].rearrange("p (s j) -> p s j", j=KT)
        taps_col = vecs[:, 128:128 + TAPS * CT].rearrange("p (t c) -> p t c", c=CT)
        convb_col = vecs[:, 256:260]
        lng_col = vecs[:, 260:264]
        lnb_col = vecs[:, 264:268]

        bank = [ctx.enter_context(nc.psum_tensor(f"bank{i}", [P, 512], F32)) for i in range(8)]

        const_ready = sem("const_ready")
        c_in, c_mm = sem("c_in"), sem("c_mm")
        vec_in = sem("vec_in")
        vec_mm = sem("vec_mm")
        vec_ready = sem("vec_ready")
        thc_done = sem("thc_done")
        x0_in = sem("x0_in")
        x0b_in = sem("x0b_in")
        ada0_in = [sem(f"ada0_in{i}") for i in range(6)]
        ada_in = [sem(f"ada_in{i}") for i in range(2)]
        ada_used = sem("ada_used")
        ada_mm = sem("ada_mm")
        ada_col = sem("ada_col")
        amul_ready = sem("amul_ready")
        raw0_in = sem("raw0_in")
        raw1_in = sem("raw1_in")
        gu_hi_r, gu_lo_r = sem("gu_hi_r"), sem("gu_lo_r")
        dn_hi_r, dn_lo_r = sem("dn_hi_r"), sem("dn_lo_r")
        gate_mm, up_mm = sem("gate_mm"), sem("up_mm")
        th_done = sem("th_done")
        gate_free, up_free = sem("gate_free"), sem("up_free")
        act_hi_r, act_lo_r = sem("act_hi_r"), sem("act_lo_r")
        down_mm = sem("down_mm")
        y_done = sem("y_done")
        root_y, root_x = sem("root_y"), sem("root_x")
        x_tile_in = [sem(f"x_tile_in{i}") for i in range(2)]
        x1_ready = sem("x1_ready")
        x_last_in = sem("x_last_in")
        last_scaled = sem("last_scaled")
        last_added = sem("last_added")
        last_done = sem("last_done")
        x1_stored = [sem(f"x1_stored{i}") for i in range(4)]
        rstd_x = sem("rstd_x")
        xhat_r = sem("xhat_r")
        t_mm = sem("t_mm")
        hf_done = sem("hf_done")
        h_hi_r, h_lo_r = sem("h_hi_r"), sem("h_lo_r")
        diag_r = sem("diag_r")
        gb_mm = sem("gb_mm")
        gb_done = sem("gb_done")
        ring_in = [sem(f"ring_in{i}") for i in range(4)]
        ring_hi, ring_lo = sem("ring_hi"), sem("ring_lo")
        gu_free = sem("gu_free")
        step_mm = sem("step_mm")
        step_act, step_dve = sem("step_act"), sem("step_dve")
        vt_mm, vt_done = sem("vt_mm"), sem("vt_done")
        conv_done = sem("conv_done")
        prod_r, prod_used = sem("prod_r"), sem("prod_used")
        mean_mm, cen_done = sem("mean_mm"), sem("cen_done")
        sq_done, var_mm = sem("sq_done"), sem("var_mm")
        lroot, ldiag = sem("lroot"), sem("ldiag")
        lb_mm = sem("lb_mm")
        yn_done = sem("yn_done")
        lth_done, lf_done = sem("lth_done"), sem("lf_done")
        c_hi_r, c_lo_r = sem("c_hi_r"), sem("c_lo_r")
        s_mm = sem("s_mm")
        s_read = sem("s_read")
        mx_r = sem("mx_r")
        rden_r = sem("rden_r")
        p_r = sem("p_r")
        pn_r = sem("pn_r")
        pT_mm, pT_r = sem("pT_mm"), sem("pT_r")
        o_mm = sem("o_mm")
        o_hi_r, o_lo_r = sem("o_hi_r"), sem("o_lo_r")
        act_self, dve_self, pool_self = sem("act_self"), sem("dve_self"), sem("pool_self")

        class Chain:

            def __init__(self, eng, s):
                self.eng, self.s, self.n = eng, s, 0

            def __call__(self, ins):
                self.n += 1
                ins.then_inc(self.s, 1)
                self.eng.wait_ge(self.s, self.n)

            def mark(self, ins):
                self.n += 1
                ins.then_inc(self.s, 1)
                return self.n

        CONV_ORDER = [CT - 1] + list(range(CT - 1))
        TILES = [t for j in CONV_ORDER for t in (("b", j), ("a", j))] + [("k", 0)] + \
                [("q", g) for g in range(QT)] + [("v", 0)]
        NIN = len(TILES)
        NOUT = TT * NB_D
        OUT0 = 2 * NIN
        RING = []
        for i in range(2 * NIN):
            RING.append(("in", i))
            if i in (5, 6, 7, 8):
                RING.append(("out", 4 + i - 5))
        RING += [("out", kt) for kt in range(4)]
        IN_AT = {i: n for n, (kind, i) in enumerate(RING) if kind == "in"}
        OUT_AT = {i: n for n, (kind, i) in enumerate(RING) if kind == "out"}

        def ring_dmas(n):
            kind, i = RING[n]
            t = TILES[i % NIN][0] if kind == "in" else None
            return 2 if t == "q" or (kind == "out" and i >= 4) else 1

        RING_COUNT = []
        seen = [0] * 4
        for n in range(len(RING)):
            seen[n % 4] += 16 * ring_dmas(n)
            RING_COUNT.append(seen[n % 4])

        def ring_dst(n):
            kind, i = RING[n]
            if kind == "in":
                return gu_hi[:, i % 4, :], gu_lo[:, i % 4, :]
            return wout_tile(i)

        def wout_tile(kt):
            if kt < 4:
                return gu_hi[:, kt, :], gu_lo[:, kt, :]
            if kt < 6:
                return act_hi[:, kt - 4, :], act_lo[:, kt - 4, :]
            return dn_hi[:, kt - 6, :], dn_lo[:, kt - 6, :]

        def ring_upto(st):
            if st + 3 < 2 * NIN:
                return IN_AT[st + 3] + 1
            return min(len(RING), IN_AT[2 * NIN - 1] + 1 + (st + 3 - 2 * NIN) + 1)

        def is_dve_step(st):
            return st < OUT0 and TILES[st % NIN][0] == "a"

        def step_reads(st):
            if is_dve_step(st):
                return step_dve, sum(is_dve_step(i) for i in range(st + 1))
            return step_act, sum(not is_dve_step(i) for i in range(st + 1))

        V_STEP = NIN - 1
        VT_STEP = (NIN, OUT0)
        VZ_STEP = 10
        SLOT0 = (NIN, OUT0)

        def chunk(st, lag):
            for half in (0, 1):
                x = st - SLOT0[half] - lag
                if 0 <= x < NCH // 2 and st < SLOT0[half] + NCH // 2 + 4:
                    return half * (NCH // 2) + x
            return None

        VT = CT - 1
        CONV_AT, PROD_AT = {}, {}

        def spread(table, half, ct, plan):
            at = 0
            for st, n in plan:
                table.setdefault(st, []).append((half, ct, at, min(TAPS, at + n)))
                at = min(TAPS, at + n)
            assert at == TAPS

        spread(CONV_AT, 0, 0, [(4, 7), (5, 7), (6, 7), (7, 8), (8, 2)])
        spread(CONV_AT, 0, 1, [(8, 5), (9, 8), (10, 7), (11, 7), (12, 4)])
        spread(CONV_AT, 0, 2, [(12, 3), (13, 7), (14, 6), (15, 5), (16, 5), (17, 5)])
        spread(CONV_AT, 1, 0, [(21, 6), (22, 8), (23, 9), (24, 8)])
        spread(CONV_AT, 1, 1, [(25, 9), (26, 9), (27, 9), (28, 4)])
        spread(CONV_AT, 1, 2, [(28, 4), (29, 9), (30, 9), (31, 9)])
        spread(PROD_AT, 0, 3, [(st, 2) for st in range(4, 7)] + [(st, 3) for st in range(7, 14)] + [(14, 4)])
        spread(PROD_AT, 1, 3, [(st, 3) for st in range(21, 27)] + [(27, 2), (28, 2), (29, 3), (30, 3), (31, 3)])
        LN0 = (18, 32)
        GATEB_STEP = 11
        NORM_B = (0, 2, 3, 4)
        TB_STEPS = (6, 7, 8, 9)
        POST_A = OUT0 + NOUT
        TA_STEPS = (41, 42)
        assert TAPS == 31 and NIN == 14 and OUT0 == 28 and LN0[1] + 3 < POST_A

        def post_y(e):
            if e in (2, 3, 6, 7):
                return [y_ffn[:, TT * (e % 2) + i, :] for i in range(TT)]
            if e == 4:
                return [raw[:, i, :] for i in range(TT)]
            return [y_ffn[:, TT + i, :] for i in range(TT)]

        def pre_x(e):
            return post_y(e) if e >= 2 else [y_ffn[:, TT * e + i, :] for i in range(TT)]

        def t_bank(e, j):
            if e == 2:
                return j if j < 4 else 2 + j % 2
            return j if e in (0, 1, 5) else 4 + j % 4

        block = ctx.enter_context(nc.Block())

        @block.sync
        def _(sp):
            sp.dma_start(vec_raw[0:8, 3 * P:4 * P], c.rearrange("b (j p) -> (b j) p", p=P)).then_inc(c_in, 16)
            sp.dma_start(vec_raw[0:72, 0:P], ada_b[0].rearrange("(r p) -> r p", p=P)).then_inc(vec_in, 16)
            sp.dma_start(vec_raw[72:96, 0:P], norm_pre[0].rearrange("s (j p) -> (s j) p", p=P)).then_inc(vec_in, 16)
            sp.dma_start(vec_raw[96:120, 0:P], norm_post[0].rearrange("s (j p) -> (s j) p", p=P)).then_inc(vec_in, 16)
            sp.dma_start(vec_raw[0:TAPS * CT, P:2 * P],
                         conv_w[0].rearrange("t o (c p) -> (t o c) p", p=P)).then_inc(vec_in, 16)
            for n, v in enumerate((conv_b, ln_g, ln_b)):
                sp.dma_start(vec_raw[4 * n:4 * n + 4, 2 * P:3 * P],
                             v.rearrange("b (j p) -> (b j) p", p=P)).then_inc(vec_in, 16)
            with nc.allow_non_contiguous_dma(reason="sinks of a head on its 64 rows"):
                for hh in range(2):
                    sp.dma_start(sink_col[64 * hh:64 * hh + 64, :],
                                 sinks.rearrange("a (i h) -> a h i", h=2)[:, hh, :].to_broadcast([64, 4])
                                 ).then_inc(vec_in, 16)

            def ada_row(m, kt):
                return ada_w[0, kt * P:(kt + 1) * P, bass.ds(m * D, D)]

            for n in range(2 * KT):
                m, kt = n // KT, n % KT
                if n >= 6:
                    sp.wait_ge(ada_used, n - 5)
                sp.dma_start(ada_start[n % 6], ada_row(m, kt)).then_inc(ada0_in[n % 6], 16)

            def load_gu(s, g, which):
                w = ffn_w[s][which].rearrange("(k p) f -> p k f", p=P)
                dst = raw[:, 2 * which:2 * which + 2, :].rearrange("p a b -> p (a b)")
                dst = dst.rearrange("p (k f) -> p k f", k=KT)
                src = w[:, :, bass.ds(g * (FG * P), FG * P)]
                return dst, src, (raw0_in, raw1_in)[which]

            def load_dn(s, g):
                w = ffn_w[s][2][bass.ds(g * (FG * P), FG * P), :].rearrange("(f p) d -> p f d", p=P)
                return raw[:, 0:FG, :], w, raw0_in

            def start(x):
                dst, src, s = x
                sp.dma_start(dst, src).then_inc(s, 16)

            start(load_gu(0, 0, 0))
            start(load_gu(0, 0, 1))
            sp.wait_ge(ada_used, 2 * KT)
            for t in range(TT, 2 * TT):
                sp.dma_start(y_ffn[:, t, :], x_tok[t]).then_inc(x0b_in, 16)

            def ada_pair(m, kt):
                for k in (kt, kt + 1):
                    src = ada_row(m, k)
                    sp.wait_ge(ada_used, m * KT + k - 1)
                    sp.dma_start(xring[:, k % 2, :], src).then_inc(ada_in[k % 2], 16)

            def ffn_group(s, G, g, ada, last, norm=None):
                dn = load_dn(s, g)
                if not last:
                    up, gate = load_gu(s, g + 1, 1), load_gu(s, g + 1, 0)
                sp.wait_ge(gu_lo_r, 4 * G + 4)
                start(dn)
                if ada:
                    ada_pair(g + 1, 2)
                if norm is not None:
                    norm()
                if not last:
                    start(up)
                if ada:
                    ada_pair(g + 1, 4)
                    ada_pair(g + 1, 6)
                if not last:
                    sp.wait_ge(dn_lo_r, G + 1)
                    start(gate)
                if ada == "next":
                    ada_pair(g + 2, 0)

            def ffn(s, G0):
                ffn_group(s, G0, 0, False, False, (lambda: post_dmas(5, False)) if s else None)
                if s == 0:
                    ada_pair(2, 0)
                    with sp.Fori(1, NM - 2) as g:
                        ffn_group(0, g, g, "next", False)
                    ffn_group(0, NM - 2, NM - 2, True, False)
                    with sp.Fori(NM - 1, LAST) as g:
                        ffn_group(0, g, g, False, False)
                else:
                    with sp.Fori(1, LAST) as g:
                        ffn_group(1, g + G2, g, False, False)
                ffn_group(s, G0 + LAST, LAST, False, True)

            def load_x(e, i):
                n = 4 * (e - 2) + i
                if n >= 2:
                    sp.wait_ge(x1_ready, n - 1)
                src = x_tok[TT * (e % 2) + i] if e < 4 else out_tok[TT * (e % 2) + i]
                if e >= 4:
                    sp.wait_ge(x1_stored[i], 16 * (e - 3))
                sp.dma_start(xring[:, n % 2, :], src).then_inc(x_tile_in[n % 2], 16)

            def store_x(e, i):
                if e < 7:
                    sp.wait_ge(x1_ready, 4 * (e - 2) + i + 1)
                elif i < TT - 1:
                    sp.wait_ge(last_added, i + 1)
                else:
                    sp.wait_ge(last_done, 1)
                sp.dma_start(out_tok[TT * (e % 2) + i], post_y(e)[i]).then_inc(x1_stored[i], 16)

            def post_dmas(e, begin=True):
                if begin:
                    load_x(e, 0)
                    load_x(e, 1)
                for i in range(TT):
                    store_x(e, i)
                    if i + 2 < TT:
                        load_x(e, i + 2)

            def load_ring(n):
                kind, i = RING[n]
                dst = raw[:, n % 4, :]
                s = ring_in[n % 4]
                if kind == "in":
                    t, j = TILES[i % NIN]
                    wv = w_in[0].rearrange("(k p) n -> p k n", p=P)
                    dv = dst.rearrange("p (k n) -> p k n", k=KT)
                    if t == "q":
                        for kv in range(2):
                            col = 2 * CONV + (kv * QT + j) * HD
                            sp.dma_start(dv[:, :, kv * HD:(kv + 1) * HD], wv[:, :, col:col + HD]).then_inc(s, 16)
                    else:
                        col = {"a": j * P, "b": CONV + j * P, "k": 2 * CONV + NH * HD,
                               "v": 2 * CONV + NH * HD + P}[t]
                        sp.dma_start(dv, wv[:, :, col:col + P]).then_inc(s, 16)
                elif i < 4:
                    sp.dma_start(dst, w_out[0, i * P:(i + 1) * P, :]).then_inc(s, 16)
                else:
                    for kv in range(2):
                        row = CONV + (kv * QT + i - 4) * HD
                        sp.dma_start(dst[kv * HD:(kv + 1) * HD, :], w_out[0, row:row + HD, :]).then_inc(s, 16)

            ffn(0, 0)
            sp.wait_ge(dn_lo_r, LAST + 1)
            load_ring(0)
            load_ring(1)
            load_ring(2)
            load_ring(3)
            sp.wait_ge(ada_used, NM * KT)
            post_dmas(2)
            for n in range(4, len(RING)):
                sp.wait_ge(ring_lo, n - 3)
                load_ring(n)
                if n == 4:
                    load_x(3, 0)
                    load_x(3, 1)
                if n == 7:
                    for i in range(2):
                        store_x(3, i)
                        load_x(3, i + 2)
                if n == 8:
                    store_x(3, 2)
                    store_x(3, 3)
            sp.wait_ge(c_lo_r, 2 * CT)
            post_dmas(4)
            load_x(5, 0)
            load_x(5, 1)
            sp.wait_ge(t_mm, 8 * 5)
            start(load_gu(1, 0, 0))
            start(load_gu(1, 0, 1))
            ffn(1, G2)
            post_dmas(6)
            sp.wait_ge(dn_lo_r, 2 * NG)
            for i in range(TT):
                sp.wait_ge(x1_stored[i], 16 * 4)
                sp.dma_start(raw[:, i, :], out_tok[TT + i]).then_inc(x_last_in, 16)
            for i in range(TT):
                store_x(7, i)
            for i in range(TT):
                sp.wait_ge(x1_stored[i], 16 * 6)

        @block.gpsimd
        def _(pool):
            one = Chain(pool, pool_self)
            pool.memset(ones[:, :], 1.0)
            pool.memset(eps_col[:, :], EPS)
            one(pool.memset(ident[:, :], 0.0))
            one(pool.affine_select(out=ident[:, :], in_=ident[:, :], compare_op=ALU.not_equal, fill=1.0,
                                   base=0, pattern=[[-1, P]], channel_multiplier=1))
            for hh in range(2):
                pool.iota(alibi[64 * hh:64 * hh + 64, 0, 3, :], pattern=[[-1, P]], base=CH, channel_multiplier=1,
                          allow_small_or_imprecise_dtypes=True).then_inc(const_ready, 1)

            def ring_lo_part(n):
                pool.wait_ge(ring_hi, n + 1)
                hi, lo = ring_dst(n)
                nc.gpsimd.tensor_tensor(lo, raw[:, n % 4, :], hi.bitcast(F32), ALU.subtract).then_inc(ring_lo, 1)

            def conv_sum(half, ct, first, end):
                for tap in range(first, end):
                    if tap == 0:
                        continue
                    n = half * (TAPS - 1) + tap
                    pool.wait_ge(prod_r, half * TAPS + tap + 1)
                    if n > 1:
                        pool.wait_ge(prod_used, n - 1)
                    nc.gpsimd.tensor_tensor(acc[ct], acc[ct], prod[n % 4],
                                            ALU.add).then_inc(prod_used, 1)

            done = 0
            for st in range(OUT0 + 2 * NOUT):
                while done < ring_upto(st):
                    ring_lo_part(done)
                    done += 1
                for a in PROD_AT.get(st, []):
                    conv_sum(*a)
            for i in range(TT - 1):
                y = post_y(7)[i]
                pool.wait_ge(last_scaled, i + 1)
                pool.wait_ge(x_last_in, 16 * TT)
                nc.gpsimd.tensor_tensor(y, y, raw[:, i, :], ALU.add).then_inc(last_added, 1)

        @block.scalar
        def _(act):
            one = Chain(act, act_self)

            def split_hi(dst, src, s):
                nc.scalar.activation(dst, src, ACT.Copy).then_inc(s, 1)

            def post_stats(e, first=0, end=TT):
                ys = post_y(e)
                if e >= 3:
                    act.wait_ge(x1_ready, 4 * (e - 2))
                for i in range(first, end):
                    if e in (4, 5):
                        act.wait_ge(step_act, step_reads(OUT0 + NOUT * (e % 2) + NB_D * (i + 1) - 1)[1])
                    else:
                        G = LAST if e < 4 else G2 + LAST
                        act.wait_ge(y_done, 16 * G + 8 * (e % 2) + NB_D * (i + 1))
                    to = y_ffn[:, 3, :] if e == 4 else junk(e)
                    one(nc.scalar.activation(to, ys[i], ACT.Square, accum_out=stat[:, SSQ, i:i + 1]))
                if end == TT or e == 7:
                    cols = slice(first if e == 7 else 0, end)
                    nc.scalar.activation(stat[:, ROOT, cols], stat[:, SSQ, cols], ACT.Sqrt, bias=eps_col[:, 0:1],
                                         scale=1.0 / D).then_inc(root_y, 1)

            def pre_stats(e, first=0, end=TT, root=True):
                xs = pre_x(e)
                if e < 2:
                    act.wait_ge((x0_in, x0b_in)[e], 16 * TT)
                    if e:
                        act.wait_ge(rstd_x, 1)
                for i in range(first, end):
                    if e >= 2:
                        act.wait_ge(x1_ready, 4 * (e - 2) + i + 1)
                    one(nc.scalar.activation(junk(e), xs[i], ACT.Square, accum_out=stat[:, SSQ, i:i + 1]))
                if end == TT and root:
                    pre_root()

            def pre_root():
                nc.scalar.activation(stat[:, ROOT, :], stat[:, SSQ, :], ACT.Sqrt, bias=eps_col[:, 0:1],
                                     scale=1.0 / D).then_inc(root_x, 1)

            def pre_xhat(e):
                xs = pre_x(e)
                act.wait_ge(rstd_x, e + 1)
                for i in range(TT):
                    if e >= 2:
                        act.wait_ge(x1_stored[i], 16 * (e - 1))
                    nc.scalar.activation(xs[i], xs[i], ACT.Copy, scale=stat[:, RSTDX, i:i + 1]).then_inc(xhat_r, 1)

            def h_unit(e, j):
                s, H = e // 2, e % 2
                n = 8 * e + j
                act.wait_ge(t_mm, n + 1)
                if n == 0:
                    act.wait_ge(amul_ready, 1)
                if n >= 2:
                    act.wait_ge(h_lo_r, n - 1)
                nc.scalar.activation(hf[n % 2], bank[t_bank(e, j)][:, :], ACT.Identity,
                                     bias=modcol[:, 3 * s, j:j + 1], scale=amul[:, s, j:j + 1]).then_inc(hf_done, 1)
                act.wait_ge(hf_done, n + 1)
                nc.scalar.activation(h_hi[:, j, H * HT:(H + 1) * HT], hf[n % 2], ACT.Copy).then_inc(h_hi_r, 1)

            def gateb(s):
                act.wait_ge(gb_mm, s + 1)
                if s:
                    act.wait_ge(x1_ready, 8 * s)
                for d in range(NB_D):
                    nc.scalar.activation(gate_b[:, d * 512:(d + 1) * 512], bank[6 + d][:, :], ACT.Copy).then_inc(gb_done, 1)

            def split_gu(G, f):
                for which in range(2):
                    act.wait_ge((raw0_in, raw1_in)[which], 16 * (2 * G + 1) if which == 0 else 16 * (G + 1))
                src = raw[:, :, :].rearrange("p (w a) b -> p w (a b)", w=2).rearrange("p w (k f) -> p w k f", k=KT)
                for which in range(2):
                    dst = gu_hi[:, 2 * f + which, :].rearrange("p (k f) -> p k f", k=KT)
                    split_hi(dst, src[:, which, :, f * P:(f + 1) * P], gu_hi_r)

            def split_dn(G):
                act.wait_ge(raw0_in, 16 * (2 * G + 2))
                split_hi(dn_hi[:, :, :], raw[:, 0:FG, :], dn_hi_r)

            def unit_th(G, h, f):
                n = 4 * G + 2 * h + f
                act.wait_ge(gate_mm, n + 1)
                if not (isinstance(n, int) and n == 0):
                    act.wait_ge(gate_free, n)
                nc.scalar.activation(th[:, :], bank[f][:, :], ACT.Tanh, scale=0.5).then_inc(th_done, 1)

            def unit_hi(G, h, f, used):
                n = 4 * G + 2 * h + f
                act.wait_ge(up_free, n + 1)
                if used:
                    act.wait_ge(down_mm, 16 * (G - 1) + 8 * h + 8)
                nc.scalar.activation(act_hi[:, h, f * HT:(f + 1) * HT], a_full[:, :], ACT.Copy).then_inc(act_hi_r, 1)

            def unit(G, h, f, used):
                unit_th(G, h, f)
                unit_hi(G, h, f, used)

            def middle(G):
                act.wait_ge(up_mm, 4 * G)
                split_gu(G, 1)
                unit(G, 0, 0, True)
                unit(G, 0, 1, True)
                act.wait_ge(down_mm, 16 * G)
                split_dn(G)
                unit(G, 1, 0, True)
                act.wait_ge(up_mm, 4 * G + 3)
                split_gu(G + 1, 0)
                unit(G, 1, 1, True)

            def ffn(s, G0):
                eB = 4 * s + 1
                if s:
                    post_stats(eB, TT - 1, TT)
                    act.wait_ge(step_mm, OUT0 + 2 * NOUT)
                split_gu(G0, 1)
                if s:
                    unit(G0, 0, 0, False)
                    split_dn(G0)
                    pre_stats(eB, root=False)
                    unit_th(G0, 0, 1)
                    pre_root()
                    unit_hi(G0, 0, 1, False)
                    pre_xhat(eB)
                else:
                    pre_stats(eB)
                    unit(G0, 0, 0, False)
                    pre_xhat(eB)
                    split_dn(G0)
                    unit(G0, 0, 1, False)
                for j in range(KT):
                    h_unit(eB, j)
                unit(G0, 1, 0, False)
                act.wait_ge(up_mm, 4 * G0 + 3)
                split_gu(G0 + 1, 0)
                unit(G0, 1, 1, False)
                with act.Fori(G0 + 1, G0 + LAST) as G:
                    middle(G)
                G = G0 + LAST
                act.wait_ge(up_mm, 4 * G)
                split_gu(G, 1)
                unit(G, 0, 0, True)
                act.wait_ge(down_mm, 16 * G)
                split_dn(G)
                unit(G, 0, 1, True)
                gateb(0 if s == 0 else 2)
                eA = 4 * s + 2
                post_stats(eA)
                unit(G, 1, 0, True)
                if s == 0:
                    pre_stats(eA, root=False)
                unit_th(G, 1, 1)
                if s == 0:
                    pre_root()
                unit_hi(G, 1, 1, True)
                if s == 0:
                    pre_xhat(eA)
                    for n in range(2):
                        ring_split(n)
                    for j in range(KT):
                        h_unit(eA, j)
                else:
                    post_stats(eA + 1, 0, TT - 1)
                    post_stats(eA + 1, TT - 1, TT)

            def ring_split(n):
                kind, i = RING[n]
                act.wait_ge(ring_in[n % 4], RING_COUNT[n])
                if kind == "in" and i < 4:
                    act.wait_ge(up_mm, 4 * LAST + 3 + i // 2)
                elif kind == "in":
                    act.wait_ge(step_mm, i - 3)
                elif i >= 4:
                    act.wait_ge(down_mm, 16 * NG)
                else:
                    act.wait_ge(step_mm, 2 * NIN - 3 + i)
                split_hi(ring_dst(n)[0], raw[:, n % 4, :], ring_hi)

            for t in range(TT):
                act.dma_start(y_ffn[:, t, :], x_tok[t]).then_inc(x0_in, 16)
            act.wait_ge(c_mm, 1)
            nc.scalar.activation(silu_c[:, :], bank[5][:, 0:KT], ACT.Tanh, scale=0.5).then_inc(thc_done, 1)
            act.wait_ge(const_ready, 2)
            pre_stats(0)
            pre_xhat(0)
            split_gu(0, 0)
            for j in range(KT):
                h_unit(0, j)
            ffn(0, 0)

            def step_read(st):
                act.wait_ge(step_mm, st + 1)
                b = bank[st % 2]
                if st >= OUT0:
                    u = st - OUT0
                    t, d = u // NB_D, u % NB_D
                    y = post_y(4 + t // TT)[t % TT]
                    if st == OUT0:
                        act.wait_ge(ring_lo, len(RING))
                    nc.scalar.activation(y[:, d * 512:(d + 1) * 512], b[:, :], ACT.Copy).then_inc(step_act, 1)
                    return
                half, (t, j) = st // NIN, TILES[st % NIN]
                if t == "b":
                    n = step_reads(st + 1)[1]
                    if n > 1:
                        act.wait_ge(step_dve, n - 1)
                    nc.scalar.activation(th[:, :], b[:, :], ACT.Tanh, scale=0.5).then_inc(step_act, 1)
                elif t == "k":
                    nc.scalar.activation(k_buf[:, half * HT:(half + 1) * HT], b[:, :], ACT.Copy).then_inc(step_act, 1)
                elif t == "v":
                    nc.scalar.activation(a_full[:, :], b[:, :], ACT.Copy).then_inc(step_act, 1)
                elif t == "q":
                    nc.scalar.activation(q_buf[:, :, j, :], b[:, :].rearrange("p (n t) -> p n t", t=CH), ACT.Copy,
                                         scale=float(HD) ** -0.5).then_inc(step_act, 1)

            def v_rows(half):
                act.wait_ge(vt_mm, half + 1)
                vb = bank[6][:, :].rearrange("p (t d) -> p t d", t=TT)
                if half:
                    act.wait_ge(o_mm, 8)
                    one(nc.scalar.activation(v_even[64:128, 0, :], v_odd[64:128, TT - 1, :], ACT.Copy))
                nc.scalar.activation(v_odd[:, :, :], vb, ACT.Copy)
                nc.scalar.activation(v_even[0:64, :, :], vb[0:64, :, :], ACT.Copy)
                nc.scalar.activation(v_even[64:128, 1:TT, :], vb[64:128, 0:TT - 1, :], ACT.Copy).then_inc(vt_done, 1)

            def layer_norm(half, part):
                if part == 1:
                    for ct in range(CT):
                        n = half * CT + ct
                        act.wait_ge(cen_done, n + 1)
                        if n >= 2:
                            act.wait_ge(var_mm, n - 1)
                        if n >= CT:
                            act.wait_ge(c_lo_r, CT)
                        nc.scalar.activation(xring[:, n % 2, 512:1024], acc[ct], ACT.Square).then_inc(sq_done, 1)
                if part == 2:
                    act.wait_ge(var_mm, CT * (half + 1))
                    one(nc.scalar.activation(lstat[:, 1, :], bank[3][:, 0:TT], ACT.Sqrt, bias=eps_col[:, 0:1],
                                             scale=1.0 / CONV))
                    nc.scalar.activation(lstat[:, 0, :], bank[3][:, 0:TT], ACT.Identity, bias=eps_col[:, 0:1],
                                         scale=1.0 / CONV).then_inc(lroot, 1)
                if part >= 3:
                    cts = range(2 * (part - 3), 2 * (part - 3) + 2)
                    for ct in cts:
                        n = half * CT + ct
                        act.wait_ge(yn_done, CT * half + ct + 1)
                        if n >= 2:
                            act.wait_ge(c_lo_r, n - 1)
                        z, t = swish[n % 2]
                        scaled = dict(bias=lnb_col[:, ct:ct + 1], scale=lng_col[:, ct:ct + 1])
                        nc.scalar.activation(z, acc[ct], ACT.Identity, **scaled)
                        nc.scalar.activation(t, acc[ct], ACT.Tanh, **scaled).then_inc(lth_done, 1)
                    for ct in cts:
                        n = half * CT + ct
                        act.wait_ge(lf_done, n + 1)
                        nc.scalar.activation(h_hi[:, ct, half * HT:(half + 1) * HT], swish[n % 2][1],
                                             ACT.Copy).then_inc(c_hi_r, 1)

            def conv_prod(half, ct, first, end):
                if first == 0:
                    act.wait_ge(step_dve, CT * half + 1)
                    if half:
                        act.wait_ge(c_lo_r, CT)
                for tap in range(first, end):
                    src = u_buf[:, ct, tap:tap + HT]
                    w = taps_col[:, tap, ct:ct + 1]
                    if tap == 0:
                        nc.scalar.activation(acc[ct], src, ACT.Identity, bias=convb_col[:, ct:ct + 1],
                                             scale=w).then_inc(prod_r, 1)
                    else:
                        n = half * (TAPS - 1) + tap
                        if n > 4:
                            act.wait_ge(prod_used, n - 4)
                        nc.scalar.activation(prod[n % 4], src, ACT.Copy, scale=w).then_inc(prod_r, 1)

            def attention(st):
                no, nt, nn, ns = chunk(st, 4), chunk(st, 3), chunk(st, 2), chunk(st, 1)
                if nn is not None:
                    act.wait_ge(rden_r, nn + 1)
                    s = s01[:, nn % 2, :].rearrange("p (i k) -> p i k", i=4)
                    for i in range(4):
                        last = nc.scalar.activation(s[:, i, :], s[:, i, :], ACT.Copy, scale=sm[:, nn % 2, RDEN, i:i + 1])
                    last.then_inc(pn_r, 1)
                if nt is not None:
                    act.wait_ge(pT_mm, nt + 1)
                    if nt:
                        act.wait_ge(o_mm, nt)
                    nc.scalar.activation(pT[:, :], bank[6][:, :], ACT.Copy).then_inc(pT_r, 1)
                if no is not None:
                    act.wait_ge(o_mm, no + 1)
                    nc.scalar.activation(h_hi[:, 4:8, no * CH:(no + 1) * CH],
                                         bank[7][:, 0:QT * CH].rearrange("p (g t) -> p g t", g=QT),
                                         ACT.Copy).then_inc(o_hi_r, 1)
                if ns is not None:
                    act.wait_ge(mx_r, ns + 1)
                    s = s01[:, ns % 2, :].rearrange("p (i k) -> p i k", i=4)
                    for i in range(4):
                        nc.scalar.activation(s[:, i, :], s[:, i, :], ACT.Exp, bias=sm[:, ns % 2, NEGM, i:i + 1],
                                             accum_out=sm[:, ns % 2, SUMS, i:i + 1])
                    nc.scalar.activation(sm[:, ns % 2, ES, :], sm[:, ns % 2, DIFF, :], ACT.Exp).then_inc(p_r, 1)

            done = 2
            for st in range(OUT0 + 2 * NOUT):
                while done < ring_upto(st):
                    ring_split(done)
                    done += 1
                if st == NORM_B[0]:
                    post_stats(3)
                if st == NORM_B[1]:
                    pre_stats(3, 0, 2)
                if st == NORM_B[2]:
                    pre_stats(3, 2, 4)
                if st == NORM_B[3]:
                    pre_xhat(3)
                if st in TB_STEPS:
                    for j in range(2):
                        h_unit(3, 2 * (st - TB_STEPS[0]) + j)
                if st == GATEB_STEP:
                    gateb(1)
                if st - 1 in VT_STEP:
                    v_rows(VT_STEP.index(st - 1))
                attention(st)
                for half in range(2):
                    if st - LN0[half] in (0, 1, 2, 3):
                        layer_norm(half, st - LN0[half] + 1)
                for a in PROD_AT.get(st, []):
                    conv_prod(*a)
                if st == POST_A - 1:
                    post_stats(4, 0, TT - 1)
                if st == POST_A:
                    post_stats(4, TT - 1, TT)
                if st == POST_A + 2:
                    pre_stats(4, 0, 2)
                if st == POST_A + 3:
                    pre_stats(4, 2, 3)
                if st == POST_A + 4:
                    pre_stats(4, 3, 4)
                    pre_xhat(4)
                if st in TA_STEPS:
                    for j in range(4):
                        h_unit(4, 4 * (st - TA_STEPS[0]) + j)
                if st == TA_STEPS[-1] + 1:
                    post_stats(5, 0, TT - 1)
                    act.wait_ge(gu_free, 1)
                    split_gu(G2, 0)
                step_read(st)
            ffn(1, G2)

        @block.vector
        def _(dve):
            one = Chain(dve, dve_self)
            TTo, TS, STT = nc.vector.tensor_tensor, nc.vector.tensor_scalar, nc.vector.scalar_tensor_tensor

            def f32(ap):
                return ap.bitcast(F32)

            def newton(dst, root, var, t1, t2):
                one(nc.vector.reciprocal(t1, root))
                one(TTo(t2, t1, t1, ALU.mult))
                one(TTo(t2, t2, var, ALU.mult))
                one(TS(t2, t2, -0.5, 1.5, ALU.mult, ALU.add))
                return TTo(dst, t1, t2, ALU.mult)

            def rstd(row, cols=slice(0, TT)):
                one(TS(stat[:, VAR, cols], stat[:, SSQ, cols], 1.0 / D, EPS, ALU.mult, ALU.add))
                return newton(*(stat[:, k, cols] for k in (row, ROOT, VAR, T1, T2)))

            def post(e, first, end):
                ys = post_y(e)
                if first == 0:
                    dve.wait_ge(root_y, e - 1)
                    one(rstd(RSTDY))
                    dve.wait_ge(gb_done, NB_D * ((e - 2) // 2 + 1))
                for i in range(first, end):
                    n = 4 * (e - 2) + i
                    one(STT(ys[i], ys[i], stat[:, RSTDY, i:i + 1], gate_b[:, :], ALU.mult, ALU.mult))
                    dve.wait_ge(x_tile_in[n % 2], 16 * (n // 2 + 1))
                    TTo(ys[i], ys[i], xring[:, n % 2, :], ALU.add).then_inc(x1_ready, 1)

            def post_last(i):
                y = post_y(7)[i]
                if i in (0, TT - 1):
                    dve.wait_ge(root_y, 6 if i == 0 else 7)
                    one(rstd(RSTDY, slice(0, TT - 1) if i == 0 else slice(i, TT)))
                scaled = STT(y, y, stat[:, RSTDY, i:i + 1], gate_b[:, :], ALU.mult, ALU.mult)
                if i < TT - 1:
                    scaled.then_inc(last_scaled, 1)
                else:
                    one(scaled)
                    dve.wait_ge(x_last_in, 16 * TT)
                    TTo(y, y, raw[:, i, :], ALU.add).then_inc(last_done, 1)

            def pre_rstd(e):
                dve.wait_ge(root_x, e + 1)
                rstd(RSTDX).then_inc(rstd_x, 1)

            def h_unit(e, j):
                n, H = 8 * e + j, e % 2
                dve.wait_ge(h_hi_r, n + 1)
                cols = slice(H * HT, (H + 1) * HT)
                TTo(h_lo[:, j, cols], hf[n % 2], f32(h_hi[:, j, cols]), ALU.subtract).then_inc(h_lo_r, 1)

            def gateb(s):
                if s:
                    dve.wait_ge(gb_mm, s)
                for j in range(KT):
                    ins = TS(diag[:, j * P:(j + 1) * P], ident[:, :], gcol[:, s, j:j + 1], None, ALU.mult)
                ins.then_inc(diag_r, 1)

            def mods(s):
                one(STT(amul[:, s, :], modcol[:, 3 * s + 1, :], 1.0, npre_col[:, s, :], ALU.add, ALU.mult))

            def mod_gate(s):
                one(STT(gcol[:, s, :], modcol[:, 3 * s + 2, :], RES[s], npost_col[:, s, :], ALU.mult, ALU.mult))

            def ada_rows(m, kts, row_of):
                for kt in kts:
                    src, arrived, count = row_of(kt)
                    dve.wait_ge(arrived, count)
                    if kt == 0:
                        TS(ada_acc, src, silu_c[:, 0:1], None, ALU.mult).then_inc(ada_used, 1)
                    else:
                        dve.wait_ge(ada_used, m * KT + kt)
                        STT(ada_acc, src, silu_c[:, kt:kt + 1], ada_acc, ALU.mult, ALU.add).then_inc(ada_used, 1)

            def ada_vec(m):
                dve.wait_ge(ada_mm, m + 1)
                mc = modcol[:, m, :] if isinstance(m, int) else modcol[:, bass.ds(m, 1), :]
                bc = ada_b_col[:, m, :] if isinstance(m, int) else ada_b_col[:, bass.ds(m, 1), :]
                src = bank[4][:, 0:KT] if isinstance(m, int) else bank[4][:, 0:KT].rearrange("p (a k) -> p a k", a=1)
                TTo(mc, src, bc, ALU.add).then_inc(ada_col, 1)

            def split_gu(G, f):
                src = raw[:, :, :].rearrange("p (w a) b -> p w (a b)", w=2).rearrange("p w (k f) -> p w k f", k=KT)
                for which in range(2):
                    dve.wait_ge(gu_hi_r, 4 * G + 2 * f + which + 1)
                    hi = gu_hi[:, 2 * f + which, :].rearrange("p (k f) -> p k f", k=KT)
                    lo = gu_lo[:, 2 * f + which, :].rearrange("p (k f) -> p k f", k=KT)
                    TTo(lo, src[:, which, :, f * P:(f + 1) * P], f32(hi), ALU.subtract).then_inc(gu_lo_r, 1)

            def split_dn(G):
                dve.wait_ge(dn_hi_r, G + 1)
                TTo(dn_lo[:, :, :], raw[:, 0:FG, :], f32(dn_hi[:, :, :]), ALU.subtract).then_inc(dn_lo_r, 1)

            def unit(G, h, f):
                n = 4 * G + 2 * h + f
                dve.wait_ge(th_done, n + 1)
                if not (isinstance(n, int) and n == 0):
                    dve.wait_ge(act_lo_r, n)
                STT(a_full[:, :], th[:, :], 1.0, bank[f][:, :], ALU.add, ALU.mult).then_inc(gate_free, 1)
                dve.wait_ge(up_mm, n + 1)
                dve.wait_ge(gate_free, n + 1)
                STT(a_full[:, :], a_full[:, :], 0.5, bank[2 + f][:, :], ALU.mult, ALU.mult).then_inc(up_free, 1)
                dve.wait_ge(act_hi_r, n + 1)
                cols = slice(f * HT, (f + 1) * HT)
                TTo(act_lo[:, h, cols], a_full[:, :], f32(act_hi[:, h, cols]), ALU.subtract).then_inc(act_lo_r, 1)

            def add_y(G, h, i, first):
                m = 16 * G + 8 * h + i
                t, d = TT * h + i // NB_D, i % NB_D
                y = y_ffn[:, t, d * 512:(d + 1) * 512]
                dve.wait_ge(down_mm, m + 1)
                if first:
                    nc.vector.tensor_copy(y, bank[4 + i % 4][:, :]).then_inc(y_done, 1)
                else:
                    dve.wait_ge(y_done, m - 15)
                    TTo(y, bank[4 + i % 4][:, :], y, ALU.add).then_inc(y_done, 1)

            def middle(G, ada_m, prev_first):
                def rows(k):
                    if ada_m is not None:
                        ada_rows(ada_m, range(k, k + 2), lambda kt: (
                            xring[:, kt % 2, :], ada_in[kt % 2], 16 * (4 * (ada_m - 2) + kt // 2 + 1)))

                split_gu(G, 1)
                rows(0)
                unit(G, 0, 0)
                rows(2)
                unit(G, 0, 1)
                for i in range(8):
                    add_y(G - 1, 1, i, prev_first)
                rows(4)
                split_dn(G)
                rows(6)
                unit(G, 1, 0)
                for i in range(8):
                    add_y(G, 0, i, False)
                split_gu(G + 1, 0)
                if ada_m is not None:
                    ada_vec(ada_m)
                unit(G, 1, 1)

            def ffn(s, G0):
                eB = 4 * s + 1
                if s:
                    split_gu(G0, 0)
                split_gu(G0, 1)
                if s:
                    post(eB, 0, 2)
                    unit(G0, 0, 0)
                    post(eB, 2, 4)
                    split_dn(G0)
                else:
                    pre_rstd(eB)
                    unit(G0, 0, 0)
                    split_dn(G0)
                unit(G0, 0, 1)
                if s:
                    pre_rstd(eB)
                for i in range(8):
                    add_y(G0, 0, i, True)
                    if i >= 4:
                        h_unit(eB, i - 4)
                for j in range(4, KT):
                    h_unit(eB, j)
                unit(G0, 1, 0)
                split_gu(G0 + 1, 0)
                unit(G0, 1, 1)
                if s == 0:
                    middle(1, 2, True)
                    with dve.Fori(2, NM - 1) as G:
                        middle(G, G + 1, False)
                    with dve.Fori(NM - 1, LAST) as G:
                        middle(G, None, False)
                else:
                    middle(G0 + 1, None, True)
                    with dve.Fori(G0 + 2, G0 + LAST) as G:
                        middle(G, None, False)
                G = G0 + LAST
                if s == 0:
                    dve.wait_ge(ada_col, NM)
                    for k in (1, 2):
                        mods(k)
                    for k in range(3):
                        mod_gate(k)
                split_gu(G, 1)
                gateb(0 if s == 0 else 2)
                unit(G, 0, 0)
                for i in range(8):
                    add_y(G - 1, 1, i, False)
                split_dn(G)
                unit(G, 0, 1)
                for i in range(8):
                    add_y(G, 0, i, False)
                eA = 4 * s + 2
                post(eA, 0, 2)
                unit(G, 1, 0)
                post(eA, 2, 4)
                unit(G, 1, 1)
                if s == 0:
                    pre_rstd(eA)
                if s == 0:
                    for j in range(KT):
                        h_unit(eA, j)
                        add_y(G, 1, j, False)
                else:
                    for i in range(6):
                        add_y(G, 1, i, False)
                    post_last(0)
                    for i in range(6, 8):
                        add_y(G, 1, i, False)
                    for i in range(1, TT):
                        post_last(i)

            dve.wait_ge(thc_done, 1)
            one(STT(silu_c[:, :], silu_c[:, :], 1.0, bank[5][:, 0:KT], ALU.add, ALU.mult))
            one(TS(silu_c[:, :], silu_c[:, :], 0.5, None, ALU.mult))
            for m in range(2):
                ada_rows(m, range(KT), lambda kt: (
                    ada_start[(m * KT + kt) % 6], ada0_in[(m * KT + kt) % 6], 16 * ((m * KT + kt) // 6 + 1)))
                if m == 0:
                    pre_rstd(0)
                    dve.wait_ge(vec_mm, 1)
                    for at, n in ((0, 120), (P, TAPS * CT), (2 * P, 12)):
                        last = nc.vector.tensor_copy(vecs[:, at:at + n], bank[6][:, at:at + n])
                    last.then_inc(vec_ready, 1)
                    dve.wait_ge(vec_ready, 1)
                ada_vec(m)
                dve.wait_ge(ada_col, m + 1)
            STT(amul[:, 0, :], modcol[:, 1, :], 1.0, npre_col[:, 0, :], ALU.add, ALU.mult).then_inc(amul_ready, 1)
            split_gu(0, 0)
            for j in range(KT):
                h_unit(0, j)
            one(TS(lng_col, lng_col, 0.5, None, ALU.mult))
            one(TS(lnb_col, lnb_col, 0.5, None, ALU.mult))
            one(TS(taps_col, taps_col, 0.5, None, ALU.mult))
            dve.wait_ge(const_ready, 2)
            dist = alibi[:, 0, TT - 1, :]
            one(STT(dist, dist, -1.0, dist, ALU.mult, ALU.max))
            for i in range(TT):
                for hh in range(2):
                    rows = slice(64 * hh, 64 * hh + 64)
                    slope = 2.0 ** (-8.0 * (2 * i + hh + 1) / NH)
                    TS(alibi[rows, 1, i, 0:CH], dist[rows, CH:P], -slope, None, ALU.mult)
                    one(TS(alibi[rows, 1, i, CH:P], dist[rows, 0:CH], -slope, None, ALU.mult))
                    one(TS(alibi[rows, 0, i, :], dist[rows, :], -slope, None, ALU.mult))
            ffn(0, 0)

            def glu(st, half, ct):
                n = step_reads(st)[1]
                if half == 0:
                    nc.vector.memset(u_buf[:, ct, 0:HIST], 0.0)
                else:
                    if ct == VT:
                        dve.wait_ge(prod_r, TAPS)
                    one(nc.vector.tensor_copy(u_buf[:, ct, 0:HIST], u_buf[:, ct, HT:HT + HIST]))
                dve.wait_ge(step_act, step_reads(st - 1)[1])
                dve.wait_ge(step_mm, st + 1)
                STT(u_buf[:, ct, HIST:HIST + HT], th[:, :], 1.0, bank[st % 2][:, :], ALU.add,
                    ALU.mult).then_inc(step_dve, 1)
                dve.wait_ge(step_dve, n)

            chain = [0, 0]

            def conv(half, ct, first, end):
                for tap in range(first, end):
                    src = u_buf[:, ct, tap:tap + HT]
                    w = taps_col[:, tap, ct:ct + 1]
                    b = bank[2 + tap % 2][:, :]
                    to = b
                    if tap < 2:
                        dve.wait_ge(dve_self, one.n)
                        ins = TS(b, src, w, convb_col[:, ct:ct + 1] if tap == 0 else 0.0, ALU.mult, ALU.add)
                    else:
                        dve.wait_ge(dve_self, chain[tap % 2])
                        to = acc[ct] if tap == TAPS - 1 else b
                        ins = STT(to, src, w, b, ALU.mult, ALU.add)
                    chain[tap % 2] = one.mark(ins)
                if end == TAPS:
                    dve.wait_ge(dve_self, one.n)
                    ins = TTo(acc[ct], bank[3][:, :], acc[ct], ALU.add)
                    if ct == VT - 1:
                        ins.then_inc(conv_done, 1)
                        dve.wait_ge(conv_done, 1 + half)
                    else:
                        one(ins)

            def layer_norm(half, part):
                if part == 1:
                    dve.wait_ge(mean_mm, half + 1)
                    for ct in range(CT):
                        STT(acc[ct], bank[3][:, :], -1.0 / CONV, acc[ct], ALU.mult,
                            ALU.add).then_inc(cen_done, 1)
                if part == 2:
                    dve.wait_ge(lroot, half + 1)
                    one(newton(lstat[:, 4, :], lstat[:, 1, :], lstat[:, 0, :], lstat[:, 2, :], lstat[:, 3, :]))
                    for i in range(TT):
                        ins = TS(a_full[:, i * P:(i + 1) * P], ident[:, :], lstat[:, 4, i:i + 1], None, ALU.mult)
                    ins.then_inc(ldiag, 1)
                if part == 3:
                    dve.wait_ge(lb_mm, half + 1)
                    for ct in range(CT):
                        TTo(acc[ct], bank[3][:, :], acc[ct], ALU.mult).then_inc(yn_done, 1)
                    dve.wait_ge(yn_done, CT * (half + 1))
                if part >= 3:
                    cts = range(2 * (part - 3), 2 * (part - 3) + 2)
                    for ct in cts:
                        n = half * CT + ct
                        z, t = swish[n % 2]
                        dve.wait_ge(lth_done, n + 1)
                        STT(t, t, 1.0, z, ALU.add, ALU.mult).then_inc(lf_done, 1)
                    for ct in cts:
                        n = half * CT + ct
                        dve.wait_ge(c_hi_r, n + 1)
                        cols = slice(half * HT, (half + 1) * HT)
                        TTo(h_lo[:, ct, cols], swish[n % 2][1], f32(h_hi[:, ct, cols]),
                            ALU.subtract).then_inc(c_lo_r, 1)

            def attention(st):
                no, nn, ns = chunk(st, 4), chunk(st, 2), chunk(st, 1)
                if nn is not None:
                    dve.wait_ge(p_r, nn + 1)
                    one(TTo(sm[:, nn % 2, DEN, :], sm[:, nn % 2, SUMS, :], sm[:, nn % 2, ES, :], ALU.add))
                    nc.vector.reciprocal(sm[:, nn % 2, RDEN, :], sm[:, nn % 2, DEN, :]).then_inc(rden_r, 1)
                if ns is not None:
                    s = s01[:, ns % 2, :].rearrange("p (i k) -> p i k", i=4)
                    tab = alibi[:, 1 - ns % 2, :, :]
                    if ns >= 2:
                        dve.wait_ge(pT_mm, ns - 1)
                    dve.wait_ge(s_mm, ns + 1)
                    keys = slice(0, CH if ns == 0 else P)
                    if ns == 0:
                        dve.wait_ge(gb_mm, 2)
                        one(nc.vector.memset(s[:, :, CH:P], NEG))
                    for kv in range(2):
                        sc = bank[4 + kv][:, 0:2 * P].rearrange("p (i k) -> p i k", i=2)
                        TTo(s[:, 2 * kv:2 * kv + 2, keys], sc[:, :, keys], tab[:, 2 * kv:2 * kv + 2, keys],
                            ALU.add).then_inc(s_read, 1)
                    dve.wait_ge(s_read, 2 * ns + 2)
                    one(nc.vector.tensor_reduce(sm[:, ns % 2, MX, :], s, AX.X, ALU.max))
                    one(TTo(sm[:, ns % 2, MX, :], sm[:, ns % 2, MX, :], sink_col[:, :], ALU.max))
                    TS(sm[:, ns % 2, NEGM, :], sm[:, ns % 2, MX, :], -1.0, None, ALU.mult)
                    TTo(sm[:, ns % 2, DIFF, :], sink_col[:, :], sm[:, ns % 2, MX, :], ALU.subtract).then_inc(mx_r, 1)
                if no is not None:
                    dve.wait_ge(o_hi_r, no + 1)
                    cols = slice(no * CH, (no + 1) * CH)
                    TTo(h_lo[:, 4:8, cols], bank[7][:, 0:QT * CH].rearrange("p (g t) -> p g t", g=QT),
                        f32(h_hi[:, 4:8, cols]), ALU.subtract).then_inc(o_lo_r, 1)

            for st in range(OUT0 + 2 * NOUT):
                if st == NORM_B[0]:
                    post(3, 0, 2)
                if st == NORM_B[1]:
                    post(3, 2, 4)
                if st == NORM_B[2]:
                    pre_rstd(3)
                if st in TB_STEPS:
                    for j in range(2):
                        h_unit(3, 2 * (st - TB_STEPS[0]) + j)
                if st == TB_STEPS[0] - 1:
                    gateb(1)
                if st == VZ_STEP:
                    dve.wait_ge(h_lo_r, 32)
                    one(nc.vector.memset(v_even[64:128, 0, :], 0.0))
                attention(st)
                for half in range(2):
                    if st - LN0[half] in (0, 1, 2, 3):
                        layer_norm(half, st - LN0[half] + 1)
                for a in CONV_AT.get(st, []):
                    conv(*a)
                if st == POST_A + 1:
                    post(4, 0, 2)
                if st == POST_A + 2:
                    post(4, 2, 3)
                if st == POST_A + 3:
                    post(4, 3, 4)
                if st == POST_A + TT:
                    pre_rstd(4)
                if st in TA_STEPS:
                    for j in range(4):
                        h_unit(4, 4 * (st - TA_STEPS[0]) + j)
                if st < OUT0 and TILES[st % NIN][0] == "a":
                    glu(st, st // NIN, TILES[st % NIN][1])
            ffn(1, G2)

        @block.tensor
        def _(pe):
            mm = nc.tensor.matmul

            def split_mm(dst, lhs, rhs, first, last):
                mm(dst, lhs[0], rhs[0], start=first, stop=False)
                mm(dst, lhs[0], rhs[1], start=False, stop=False)
                return mm(dst, lhs[1], rhs[0], start=False, stop=last)

            def h_cols(kt, H):
                cols = slice(H * HT, (H + 1) * HT)
                return h_hi[:, kt, cols], h_lo[:, kt, cols]

            def t_unit(e, j):
                n = 8 * e + j
                if j == 0:
                    pe.wait_ge(xhat_r, TT * (e + 1))
                t_free(e, j)
                b = bank[t_bank(e, j)]
                xs = pre_x(e)
                for i in range(TT):
                    last = nc.tensor.transpose(b[:, i * P:(i + 1) * P], xs[i][:, j * P:(j + 1) * P], ident[:, :])
                last.then_inc(t_mm, 1)

            def t_free(e, j):
                G = G2 if e == 5 else 0
                if e == 0:
                    if j >= 4:
                        pe.wait_ge(ada_col, 2)
                elif e in (1, 5):
                    if j < 4:
                        pe.wait_ge(up_free, 4 * G + 2)
                    else:
                        pe.wait_ge(y_done, 16 * G + j + 1)
                elif j >= 4:
                    pe.wait_ge(hf_done, 8 * e + j - (1 if e == 2 else 3))
                elif e == 2:
                    pe.wait_ge(up_free, 4 * NG)
                elif e == 3:
                    pe.wait_ge(y_done, 16 * NG)
                else:
                    pe.wait_ge(o_lo_r, NCH)

            def gate_up(G, h, f, ada_m=None, fresh=None):
                n = 4 * G + 2 * h + f
                for which in range(2):
                    if h == 0:
                        pe.wait_ge(gu_lo_r, 4 * G + 2 * f + which + 1)
                    if which and ada_m is not None:
                        pe.wait_ge(y_done, 16 * G + 5)
                        ada_reduce(ada_m)
                    if not (isinstance(n, int) and n < 2):
                        pe.wait_ge((gate_free, up_free)[which], n - 1)
                    w = gu_hi[:, 2 * f + which, :], gu_lo[:, 2 * f + which, :]
                    for kt in range(KT):
                        if fresh is not None and not which:
                            pe.wait_ge(h_lo_r, 8 * fresh + kt + 1)
                        k = slice(kt * P, (kt + 1) * P)
                        last = split_mm(bank[2 * which + f][:, :], (w[0][:, k], w[1][:, k]), h_cols(kt, h),
                                        kt == 0, kt == KT - 1)
                    last.then_inc((gate_mm, up_mm)[which], 1)

            def down(G, h, i):
                m = 16 * G + 8 * h + i
                if i == 0:
                    pe.wait_ge(act_lo_r, 4 * G + 2 * h + 2)
                    pe.wait_ge(dn_lo_r, G + 1)
                if not (isinstance(m, int) and m < 4):
                    pe.wait_ge(y_done, m - 3)
                t, d = i // NB_D, i % NB_D
                for f in range(FG):
                    a = slice(f * HT + t * P, f * HT + (t + 1) * P)
                    n = slice(d * 512, (d + 1) * 512)
                    last = split_mm(bank[4 + i % 4][:, :], (act_hi[:, h, a], act_lo[:, h, a]),
                                    (dn_hi[:, f, n], dn_lo[:, f, n]), f == 0, f == FG - 1)
                last.then_inc(down_mm, 1)

            def ada_reduce(m):
                pe.wait_ge(ada_used, (m + 1) * KT)
                for j in range(KT):
                    last = mm(bank[4][:, j:j + 1], ada_acc[:, j * P:(j + 1) * P], ones[:, 0:1], start=True, stop=True)
                last.then_inc(ada_mm, 1)

            def gateb(s):
                pe.wait_ge(diag_r, s + 1)
                for j in range(KT):
                    last = mm(bank[6 + j // 4][:, (j % 4) * P:(j % 4 + 1) * P], ones[:, :],
                              diag[:, j * P:(j + 1) * P], start=True, stop=True)
                last.then_inc(gb_mm, 1)

            def middle(G, s, ada_m):
                gate_up(G, 0, 0)
                gate_up(G, 0, 1)
                if s == 0:
                    pe.wait_ge(ada_col, G + 1 if ada_m is not None else NM)
                for i in range(8):
                    down(G - 1, 1, i)
                gate_up(G, 1, 0)
                for i in range(8):
                    down(G, 0, i)
                gate_up(G, 1, 1, ada_m)

            def ffn(s, G0):
                eB = 4 * s + 1
                if s:
                    pe.wait_ge(*step_reads(OUT0 + 2 * NOUT - 2))
                gate_up(G0, 0, 0, fresh=eB - 1)
                if s:
                    pe.wait_ge(*step_reads(OUT0 + 2 * NOUT - 1))
                gate_up(G0, 0, 1)
                if s:
                    pe.wait_ge(hf_done, 8 * 5)
                for i in range(8):
                    if i == 4:
                        for j in range(4):
                            t_unit(eB, j)
                    down(G0, 0, i)
                for j in range(4, KT):
                    t_unit(eB, j)
                gate_up(G0, 1, 0, fresh=eB)
                gate_up(G0, 1, 1)
                if s == 0:
                    with pe.Fori(1, NM - 1) as G:
                        middle(G, 0, G + 1)
                    with pe.Fori(NM - 1, LAST) as G:
                        middle(G, 0, None)
                else:
                    with pe.Fori(G0 + 1, G0 + LAST) as G:
                        middle(G, 1, None)
                G = G0 + LAST
                gate_up(G, 0, 0)
                for i in range(8):
                    down(G - 1, 1, i)
                gate_up(G, 0, 1)
                pe.wait_ge(y_done, 16 * G)
                gateb(0 if s == 0 else 2)
                for i in range(8):
                    if i == 2:
                        pe.wait_ge(gb_done, 2 if s == 0 else 6)
                    down(G, 0, i)
                gate_up(G, 1, 0)
                gate_up(G, 1, 1)
                for i in range(4):
                    down(G, 1, i)
                if s == 0:
                    for j in range(4):
                        t_unit(2, j)
                for i in range(4, 8):
                    down(G, 1, i)
                    if s == 0 and i > 4:
                        t_unit(2, i - 1)
                if s == 0:
                    t_unit(2, KT - 1)

            pe.wait_ge(c_in, 16)
            pe.wait_ge(pool_self, 2)
            nc.tensor.transpose(bank[5][:, 0:8], vec_raw[0:8, 3 * P:4 * P], ident[0:8, 0:8]).then_inc(c_mm, 1)
            pe.wait_ge(vec_in, 16 * 9)
            for n, rows in enumerate((120, TAPS * CT, 12)):
                last = nc.tensor.transpose(bank[6][:, n * P:n * P + rows], vec_raw[0:rows, n * P:(n + 1) * P],
                                           ident[0:rows, 0:rows])
            last.then_inc(vec_mm, 1)
            for m in range(2):
                if m:
                    pe.wait_ge(ada_col, m)
                ada_reduce(m)
                for j in range(4 * m, 4 * m + 4):
                    t_unit(0, j)
            ffn(0, 0)

            def project(st):
                half, (t, j) = st // NIN, TILES[st % NIN]
                pe.wait_ge(ring_lo, IN_AT[st] + 1)
                if st >= 2:
                    pe.wait_ge(*step_reads(st - 2))
                if st == NIN:
                    pe.wait_ge(h_lo_r, 8 * 4)
                for kt in range(KT):
                    if st == 0:
                        pe.wait_ge(h_lo_r, 8 * 2 + kt + 1)
                    k = slice(kt * P, (kt + 1) * P)
                    w = gu_hi[:, st % 4, k], gu_lo[:, st % 4, k]
                    last = split_mm(bank[st % 2][:, :], w, h_cols(kt, half), kt == 0, kt == KT - 1)
                last.then_inc(step_mm, 1)

            def mix_out(st):
                u = st - OUT0
                t, d = u // NB_D, u % NB_D
                n = slice(d * 512, (d + 1) * 512)
                pe.wait_ge(*step_reads(st - 2))
                last_step = st == OUT0 + 2 * NOUT - 1
                order = [0, 1, 2, 3, 4, 5, 6, 7] if last_step else [4, 5, 6, 7, 0, 1, 2, 3]
                for k, kt in enumerate(order):
                    pe.wait_ge(ring_lo, OUT_AT[kt] + 1)
                    if kt == 4:
                        pe.wait_ge(o_lo_r, 2 * t + 2)
                    if kt < CT:
                        pe.wait_ge(c_lo_r, CT * (t // TT) + kt + 1)
                    rows = slice(t * P, (t + 1) * P)
                    w = wout_tile(kt)
                    last = split_mm(bank[st % 2][:, :], (h_hi[:, kt, rows], h_lo[:, kt, rows]),
                                    (w[0][:, n], w[1][:, n]), k == 0, k == KT - 1)
                    if last_step and kt == 1:
                        last.then_inc(gu_free, 1)
                last.then_inc(step_mm, 1)

            def v_rows(half):
                pe.wait_ge(step_act, step_reads(half * NIN + V_STEP)[1])
                if half:
                    pe.wait_ge(pT_r, NCH // 2)
                for i in range(TT):
                    last = nc.tensor.transpose(bank[6][:, i * P:(i + 1) * P], a_full[:, i * P:(i + 1) * P], ident[:, :])
                last.then_inc(vt_mm, 1)

            def attention(st):
                no, nt = chunk(st, 4), chunk(st, 3)
                if no is not None:
                    pe.wait_ge(pT_r, no + 1)
                    if no:
                        pe.wait_ge(o_lo_r, no)
                    v = v_odd[:, ((no - 1) // 2) % TT, :] if no % 2 else v_even[:, (no // 2) % TT, :]
                    for kv in range(2):
                        last = mm(bank[7][kv * HD:(kv + 1) * HD, 0:2 * P], v[:, kv * HD:(kv + 1) * HD],
                                  pT[:, kv * 2 * P:(kv + 1) * 2 * P], start=True, stop=True)
                    last.then_inc(o_mm, 1)
                if nt is not None:
                    pe.wait_ge(pn_r, nt + 1)
                    pe.wait_ge(vt_done, nt // 8 + 1)
                    if nt:
                        pe.wait_ge(pT_r, nt)
                    for i in range(4):
                        last = nc.tensor.transpose(bank[6][:, i * P:(i + 1) * P],
                                                   s01[:, nt % 2, i * P:(i + 1) * P], ident[:, :])
                    last.then_inc(pT_mm, 1)

            def scores(st):
                ns = chunk(st, 0)
                if ns is not None:
                    pe.wait_ge(step_act, step_reads((ns // 8) * NIN + NIN - 2)[1])
                    if ns:
                        pe.wait_ge(s_read, 2 * ns)
                    for i in range(4):
                        kv, g0 = i // 2, 2 * (i % 2)
                        rows = slice(kv * HD, (kv + 1) * HD)
                        q = q_buf[rows, ns % 8, g0:g0 + 2, :].rearrange("p g t -> p (g t)")
                        col = (i % 2) * P
                        if ns % 2:
                            parts = [(slice(col, col + P), slice((ns - 1) * CH, (ns + 1) * CH))]
                        else:
                            parts = [(slice(col, col + CH), slice(ns * CH, (ns + 1) * CH))]
                            if ns:
                                parts.append((slice(col + CH, col + P), slice((ns - 1) * CH, ns * CH)))
                        for to, keys in parts:
                            last = mm(bank[4 + kv][:, to], q, k_buf[rows, keys], start=True, stop=True)
                    last.then_inc(s_mm, 1)

            def layer_norm(half, part):
                if part == 0:
                    pe.wait_ge(conv_done, 1 + half)
                    pe.wait_ge(prod_used, (TAPS - 1) * (half + 1))
                    for ct in range(CT):
                        last = mm(bank[3][:, :], ones[:, :], acc[ct], start=ct == 0, stop=ct == CT - 1)
                    last.then_inc(mean_mm, 1)
                if part == 1:
                    pe.wait_ge(cen_done, CT * (half + 1))
                    for ct in range(CT):
                        pe.wait_ge(sq_done, CT * half + ct + 1)
                        n = (half * CT + ct) % 2
                        for i in range(TT):
                            last = mm(bank[3][:, i:i + 1], xring[:, n, 512 + i * P:512 + (i + 1) * P], ones[:, 0:1],
                                      start=ct == 0 and i == 0, stop=ct == CT - 1 and i == TT - 1,
                                      skip_group_check=True)
                        last.then_inc(var_mm, 1)
                if part == 2:
                    pe.wait_ge(ldiag, half + 1)
                    for i in range(TT):
                        last = mm(bank[3][:, i * P:(i + 1) * P], ones[:, :], a_full[:, i * P:(i + 1) * P],
                                  start=True, stop=True)
                    last.then_inc(lb_mm, 1)

            for st in range(OUT0 + 2 * NOUT):
                attention(st)
                for half in range(2):
                    if st - LN0[half] in (0, 1, 2):
                        layer_norm(half, st - LN0[half])
                if st in TB_STEPS:
                    for j in range(2):
                        t_unit(3, 2 * (st - TB_STEPS[0]) + j)
                if st == GATEB_STEP:
                    pe.wait_ge(hf_done, 8 * 4)
                    gateb(1)
                if st in TA_STEPS:
                    for j in range(4):
                        t_unit(4, 4 * (st - TA_STEPS[0]) + j)
                if st < OUT0:
                    project(st)
                else:
                    mix_out(st)
                if st in VT_STEP:
                    v_rows(VT_STEP.index(st))
                scores(st)
            ffn(1, G2)


_INS = ["x", "c", "ada_w", "ada_b", "norm_pre", "norm_post",
        "ffn1_w_gate", "ffn1_w_up", "ffn1_w_down", "ffn2_w_gate", "ffn2_w_up", "ffn2_w_down",
        "mix_w_in", "conv_w", "conv_b", "conv_ln_g", "conv_ln_b", "attn_sinks", "mix_w_out"]


def kernel(**inputs):
    import numpy as _np
    import concourse.bacc as _bacc
    from concourse import mybir as _mybir
    from concourse.bass_utils import run_bass_kernel_spmd as _run

    nc = _bacc.Bacc("TRN2", target_bir_lowering=False, num_devices=1)
    arrays, args = {}, []
    for name in _INS:
        a = _np.ascontiguousarray(inputs[name])
        arrays[f"in_{name}_dram"] = a
        args.append(nc.dram_tensor(f"in_{name}_dram", a.shape, _mybir.dt.from_np(a.dtype), kind="ExternalInput").ap())
    args.append(nc.dram_tensor("out_dram", arrays["in_x_dram"].shape, _mybir.dt.float32, kind="ExternalOutput").ap())
    layer(nc, *args)
    r = _run(nc, [arrays], core_ids=[0])
    return r.results[0]["out_dram"]
```
